# Optimizing a Trainium2 kernel written in Bass

```python
import jax
import jax.numpy as jnp
from jax import lax
import numpy as np

D_MODEL = 1024
BATCH = 1
SEQ = 128
DEPTH = 2
DEC_BATCH = 1
DEC_SEQ = 512
PAST_LEN = 128

GRID_W = 64
EPS = 1e-6
HG_HEADS = 8
HG_DK = 64
HG_DV = 64
HG_CHUNK = 32
FORGET_FLOOR = 1e-6
MLA_HEADS = 8
MLA_Q_LORA = 384
MLA_KV_LORA = 256
MLA_NOPE = 64
MLA_ROPE = 32
MLA_V = 64
MLA_SCALE = (MLA_NOPE + MLA_ROPE) ** -0.5
ROPE_AXIS_DIM = MLA_ROPE // 2
ROPE_BASE = 10000.0
Q_BLOCK = 128
MIX_WIDTH = HG_HEADS * HG_DV + MLA_HEADS * MLA_V
IN_WIDTHS = (HG_HEADS * HG_DK, HG_HEADS * HG_DK, HG_HEADS * HG_DK, HG_HEADS * HG_DV, HG_HEADS * HG_DV, MLA_Q_LORA, MLA_KV_LORA, MLA_ROPE)
IN_WIDTH = 3 * HG_HEADS * HG_DK + 2 * HG_HEADS * HG_DV + MLA_Q_LORA + MLA_KV_LORA + MLA_ROPE
PEER_HEADS = 8
PEER_NKEYS = 128
PEER_EXPERTS = PEER_NKEYS * PEER_NKEYS
PEER_DQ = 256
PEER_TOPK = 16
TOK_BLOCK = 128

kernel_name = 'hymba_hgrn2_mla_peer_diffusion_step'

def rmsnorm(x, g):
    xf = x.astype(jnp.float32)
    y = xf * lax.rsqrt(jnp.mean(xf * xf, axis=-1, keepdims=True) + EPS)
    return (y * g.astype(jnp.float32)).astype(x.dtype)

def hgrn_lower_bounds(logits):
    p = jax.nn.softmax(logits.astype(jnp.float32), axis=1)
    return jnp.cumsum(p, axis=1) - p[:, :1]

def log_forget(z, lb):
    B, L, _ = z.shape
    zf = z.astype(jnp.float32).reshape(B, L, HG_HEADS, HG_DK)
    lb = lb.reshape(HG_HEADS, HG_DK)
    f = lb + (1.0 - lb) * jax.nn.sigmoid(zf)
    return jnp.log(jnp.maximum(f, FORGET_FLOOR))

def chunk_gla(q, logf, v, S0):
    B, L, H, dk = q.shape
    dv = v.shape[-1]
    n_chunks = L // HG_CHUNK
    k = -jnp.expm1(logf)

    def to_chunks(t):
        return jnp.moveaxis(t.astype(jnp.float32).reshape(B, n_chunks, HG_CHUNK, H, t.shape[-1]), 1, 0)

    mask = jnp.tril(jnp.ones((HG_CHUNK, HG_CHUNK), dtype=bool))[None, :, :, None, None]

    def step(S, inp):
        qc, gc, kc, vc = inp
        b = jnp.cumsum(gc, axis=1)
        o_inter = jnp.einsum('bthk,bhkv->bthv', qc * jnp.exp(b), S)
        diff = b[:, :, None] - b[:, None, :]
        decay = jnp.where(mask, jnp.exp(jnp.where(mask, diff, 0.0)), 0.0)
        A = jnp.einsum('bthk,btshk,bshk->bhts', qc, decay, kc)
        o_intra = jnp.einsum('bhts,bshv->bthv', A, vc)
        b_end = b[:, -1]
        S_new = jnp.exp(b_end)[..., None] * S + jnp.einsum('bshk,bshv->bhkv', kc * jnp.exp(b_end[:, None] - b), vc)
        return S_new, o_inter + o_intra

    S_final, o = lax.scan(step, S0.astype(jnp.float32), (to_chunks(q), to_chunks(logf), to_chunks(k), to_chunks(v)))
    return jnp.moveaxis(o, 0, 1).reshape(B, L, H, dv), S_final

def axial_rope_tables(L):
    rows = L // GRID_W
    row = jnp.broadcast_to(jnp.arange(rows)[:, None], (rows, GRID_W)).reshape(L).astype(jnp.float32)
    col = jnp.broadcast_to(jnp.arange(GRID_W)[None, :], (rows, GRID_W)).reshape(L).astype(jnp.float32)
    inv = 1.0 / (ROPE_BASE ** (jnp.arange(0, ROPE_AXIS_DIM, 2, dtype=jnp.float32) / ROPE_AXIS_DIM))
    ang = jnp.concatenate([row[:, None] * inv, col[:, None] * inv], axis=-1)
    return jnp.cos(ang), jnp.sin(ang)

def apply_axial_rope(x, cos, sin):
    half = ROPE_AXIS_DIM // 2
    xr = x.astype(jnp.float32).reshape(x.shape[:-1] + (2, 2, half))
    x1, x2 = xr[..., 0, :], xr[..., 1, :]
    c = cos.reshape(cos.shape[:-1] + (2, half))
    s = sin.reshape(sin.shape[:-1] + (2, half))
    out = jnp.stack([x1 * c - x2 * s, x1 * s + x2 * c], axis=-2)
    return out.reshape(x.shape).astype(x.dtype)

def attend(q_nope, q_pe, k_nope, k_pe, v):
    B, Lq, H, _ = q_nope.shape
    nb = Lq // Q_BLOCK

    def to_blocks(t):
        return jnp.moveaxis(t.reshape(B, nb, Q_BLOCK, H, t.shape[-1]), 1, 0)

    def block(args):
        qn, qp = args
        s = jnp.einsum('bqhd,bkhd->bhqk', qn, k_nope) + jnp.einsum('bqhr,bkr->bhqk', qp, k_pe)
        p = jax.nn.softmax(s.astype(jnp.float32) * MLA_SCALE, axis=-1)
        return jnp.einsum('bhqk,bkhd->bqhd', p.astype(v.dtype), v)

    o = lax.map(block, (to_blocks(q_nope), to_blocks(q_pe)))
    return jnp.moveaxis(o, 0, 1).reshape(B, Lq, H * v.shape[-1])

def mla_kv_up(ckv, w_kvb):
    B, L, _ = ckv.shape
    kv = (ckv @ w_kvb).reshape(B, L, MLA_HEADS, MLA_NOPE + MLA_V)
    return kv[..., :MLA_NOPE], kv[..., MLA_NOPE:]

def peer(h, w_q, sub_keys, u, v):
    B, L, D = h.shape
    tokens = h.reshape(B * L // TOK_BLOCK, TOK_BLOCK, D)
    k1 = sub_keys[0].astype(jnp.float32)
    k2 = sub_keys[1].astype(jnp.float32)

    def block(xb):
        q = (xb @ w_q).astype(jnp.float32).reshape(TOK_BLOCK, PEER_HEADS, 2, PEER_DQ // 2)
        s1 = jnp.einsum('thd,hkd->thk', q[:, :, 0], k1)
        s2 = jnp.einsum('thd,hkd->thk', q[:, :, 1], k2)
        v1, i1 = lax.top_k(s1, PEER_TOPK)
        v2, i2 = lax.top_k(s2, PEER_TOPK)
        cand_s = (v1[..., :, None] + v2[..., None, :]).reshape(TOK_BLOCK, PEER_HEADS, PEER_TOPK * PEER_TOPK)
        cand_i = (i1[..., :, None] * PEER_NKEYS + i2[..., None, :]).reshape(TOK_BLOCK, PEER_HEADS, PEER_TOPK * PEER_TOPK)
        best_s, best_pos = lax.top_k(cand_s, PEER_TOPK)
        idx = jnp.take_along_axis(cand_i, best_pos, axis=-1)
        gate = jax.nn.softmax(best_s, axis=-1)
        ue = u[idx]
        act = jax.nn.gelu(jnp.einsum('td,thkd->thk', xb, ue).astype(jnp.float32), approximate=False)
        ve = v[idx]
        return jnp.einsum('thk,thkd->td', (gate * act).astype(xb.dtype), ve)

    out = lax.map(block, tokens)
    return out.reshape(B, L, D)

def trunk_layer(x, cond, l, P, lb, ctx):
    B, L, _ = x.shape
    mod = jax.nn.silu(cond) @ P['w_ada'][l] + P['b_ada'][l]
    mod = mod[None, None] if cond.ndim == 1 else mod[:, None]
    shift1, scale1, gate1, shift2, scale2, gate2 = jnp.split(mod, 6, axis=-1)

    h = rmsnorm(x, P['norm_mix'][l]) * (1 + scale1) + shift1
    proj = h @ P['w_in'][l]
    split_points = [int(s) for s in np.cumsum(np.array(IN_WIDTHS))[:-1]]
    hq, hff, hfb, hi, hgt, cq, ckv_raw, kpe = jnp.split(proj, split_points, axis=-1)

    q = hq.reshape(B, L, HG_HEADS, HG_DK) * (HG_DK ** -0.5)
    logf_f = log_forget(hff, lb[0, l])
    logf_b = log_forget(hfb, lb[1, l])
    v_in = hi.reshape(B, L, HG_HEADS, HG_DV)
    if ctx is None:
        S0_f = jnp.zeros((B, HG_HEADS, HG_DK, HG_DV), jnp.float32)
        S0_b = S0_f
    else:
        S0_f = ctx[2][:, 0]
        S0_b = ctx[2][:, 1]
    o_f, S_f = chunk_gla(q, logf_f, v_in, S0_f)
    o_b, S_b = chunk_gla(q[:, ::-1], logf_b[:, ::-1], v_in[:, ::-1], S0_b)
    o = rmsnorm(o_f + o_b[:, ::-1], P['hgrn_norm'][l]) * jax.nn.silu(hgt.reshape(B, L, HG_HEADS, HG_DV).astype(jnp.float32))
    hg_out = o.reshape(B, L, HG_HEADS * HG_DV).astype(x.dtype)

    cq = rmsnorm(cq, P['mla_q_norm'][l])
    qf = (cq @ P['mla_wqb'][l]).reshape(B, L, MLA_HEADS, MLA_NOPE + MLA_ROPE)
    q_nope, q_pe = qf[..., :MLA_NOPE], qf[..., MLA_NOPE:]
    ckv = rmsnorm(ckv_raw, P['mla_kv_norm'][l])
    k_nope, v_att = mla_kv_up(ckv, P['mla_wkvb'][l])
    if ctx is None:
        attn = attend(q_nope, q_pe, k_nope, kpe, v_att)
        new_ctx = (ckv, kpe, jnp.stack([S_f, S_b], axis=1))
    else:
        cos, sin = axial_rope_tables(L)
        q_pe = apply_axial_rope(q_pe, cos[:, None], sin[:, None])
        kpe_lat = apply_axial_rope(kpe, cos, sin)
        kn_c, v_c = mla_kv_up(ctx[0], P['mla_wkvb'][l])
        attn = attend(q_nope, q_pe,
                      jnp.concatenate([kn_c.astype(k_nope.dtype), k_nope], axis=1),
                      jnp.concatenate([ctx[1].astype(kpe_lat.dtype), kpe_lat], axis=1),
                      jnp.concatenate([v_c.astype(v_att.dtype), v_att], axis=1))
        new_ctx = None

    mix = jnp.concatenate([hg_out, attn.astype(x.dtype)], axis=-1) @ P['w_out'][l]
    x = x + gate1 * mix

    h2 = rmsnorm(x, P['norm_ffn'][l]) * (1 + scale2) + shift2
    x = x + gate2 * peer(h2, P['peer_wq'][l], P['peer_keys'][l], P['peer_u'][l], P['peer_v'][l])
    return x, new_ctx

def setup_inputs(seed: int = 0) -> dict:
    key = jax.random.key(seed)
    ks = jax.random.split(key, 24)
    nrm = jax.random.normal
    D = D_MODEL
    f32 = jnp.float32
    return {
        'x_prompt': nrm(ks[0], (BATCH, SEQ, D), f32),
        'x_sample': nrm(ks[1], (DEC_BATCH, DEC_SEQ, D), f32),
        'cache_ckv': nrm(ks[2], (DEC_BATCH, DEPTH, PAST_LEN, MLA_KV_LORA), f32),
        'cache_kpe': nrm(ks[3], (DEC_BATCH, DEPTH, PAST_LEN, MLA_ROPE), f32),
        'state_hgrn': 0.5 * nrm(ks[4], (DEC_BATCH, DEPTH, 2, HG_HEADS, HG_DK, HG_DV), f32),
        'c': nrm(ks[5], (DEC_BATCH, D), f32),
        'c_ctx': nrm(ks[6], (D,), f32),
        'w_ada': 0.5 * D ** -0.5 * nrm(ks[7], (DEPTH, D, 6 * D), f32),
        'b_ada': 0.01 * nrm(ks[8], (DEPTH, 6 * D), f32),
        'norm_mix': 1.0 + 0.02 * nrm(ks[9], (DEPTH, D), f32),
        'w_in': D ** -0.5 * nrm(ks[10], (DEPTH, D, IN_WIDTH), f32),
        'hgrn_lb_logits': 0.5 * nrm(ks[11], (2, DEPTH, HG_HEADS * HG_DK), f32),
        'hgrn_norm': 1.0 + 0.02 * nrm(ks[12], (DEPTH, HG_DV), f32),
        'mla_q_norm': 1.0 + 0.02 * nrm(ks[13], (DEPTH, MLA_Q_LORA), f32),
        'mla_wqb': MLA_Q_LORA ** -0.5 * nrm(ks[14], (DEPTH, MLA_Q_LORA, MLA_HEADS * (MLA_NOPE + MLA_ROPE)), f32),
        'mla_kv_norm': 1.0 + 0.02 * nrm(ks[15], (DEPTH, MLA_KV_LORA), f32),
        'mla_wkvb': MLA_KV_LORA ** -0.5 * nrm(ks[16], (DEPTH, MLA_KV_LORA, MLA_HEADS * (MLA_NOPE + MLA_V)), f32),
        'w_out': MIX_WIDTH ** -0.5 * nrm(ks[17], (DEPTH, MIX_WIDTH, D), f32),
        'norm_ffn': 1.0 + 0.02 * nrm(ks[18], (DEPTH, D), f32),
        'peer_wq': D ** -0.5 * nrm(ks[19], (DEPTH, D, PEER_HEADS * PEER_DQ), f32),
        'peer_keys': (PEER_DQ // 2) ** -0.5 * nrm(ks[20], (DEPTH, 2, PEER_HEADS, PEER_NKEYS, PEER_DQ // 2), f32),
        'peer_u': D ** -0.5 * nrm(ks[21], (DEPTH, PEER_EXPERTS, D), f32),
        'peer_v': 0.5 * nrm(ks[22], (DEPTH, PEER_EXPERTS, D), f32),
        'final_norm': 1.0 + 0.02 * nrm(ks[23], (D,), f32),
    }

def reference(x_prompt, x_sample, cache_ckv, cache_kpe, state_hgrn, c, c_ctx,
              w_ada, b_ada, norm_mix, w_in, hgrn_lb_logits, hgrn_norm,
              mla_q_norm, mla_wqb, mla_kv_norm, mla_wkvb, w_out, norm_ffn,
              peer_wq, peer_keys, peer_u, peer_v, final_norm):
    P = {
        'w_ada': w_ada, 'b_ada': b_ada, 'norm_mix': norm_mix, 'w_in': w_in,
        'hgrn_norm': hgrn_norm, 'mla_q_norm': mla_q_norm, 'mla_wqb': mla_wqb,
        'mla_kv_norm': mla_kv_norm, 'mla_wkvb': mla_wkvb, 'w_out': w_out,
        'norm_ffn': norm_ffn, 'peer_wq': peer_wq, 'peer_keys': peer_keys,
        'peer_u': peer_u, 'peer_v': peer_v,
    }
    lb = hgrn_lower_bounds(hgrn_lb_logits)

    xp = x_prompt
    ckvs, kpes, states = [], [], []
    for l in range(DEPTH):
        xp, (ckv_l, kpe_l, st_l) = trunk_layer(xp, c_ctx, l, P, lb, None)
        ckvs.append(ckv_l)
        kpes.append(kpe_l)
        states.append(st_l)

    xs = x_sample
    for l in range(DEPTH):
        xs, _ = trunk_layer(xs, c, l, P, lb, (cache_ckv[:, l], cache_kpe[:, l], state_hgrn[:, l]))

    y_prompt = rmsnorm(xp, final_norm)
    y_sample = rmsnorm(xs, final_norm)
    new_cache_ckv = jnp.stack(ckvs, axis=1)
    new_cache_kpe = jnp.stack(kpes, axis=1)
    new_state_hgrn = jnp.stack(states, axis=1).astype(x_prompt.dtype)
    return (y_prompt, y_sample, new_cache_ckv, new_cache_kpe, new_state_hgrn)


_drawn_inputs = setup_inputs


def setup_inputs(seed=0):
    import zlib

    import numpy as np

    out = dict(_drawn_inputs(seed))
    spreads = {}
    factors = {'cache_ckv': 3.699,
     'cache_kpe': 5.31,
     'state_hgrn': 5.131,
     'b_ada': 2.905,
     'norm_mix': 2.785,
     'hgrn_norm': 6.389,
     'mla_q_norm': 8.0,
     'mla_kv_norm': 2.831,
     'norm_ffn': 9.106,
     'final_norm': 8.222}
    for name, (base, spread) in spreads.items():
        noise = np.random.default_rng([zlib.crc32(name.encode()), seed]).standard_normal(out[name].shape)
        drawn = base * np.exp(spread * noise) if base else spread * noise
        out[name] = jnp.asarray(drawn.astype(out[name].dtype))
    for name, factor in factors.items():
        out[name] = (out[name] * factor).astype(out[name].dtype)
    return out
```

```python
from contextlib import ExitStack

import numpy as np

import concourse.bass as bass
from concourse import mybir

ALU = mybir.AluOpType
ACT = mybir.ActivationFunctionType
AX = mybir.AxisListType
F32 = mybir.dt.float32
I32 = mybir.dt.int32
U32 = mybir.dt.uint32

P = 128
D = 1024
KC = D // P
DEPTH = 2
EPS = 1e-6
FLOOR = 1e-6
SEQ, DEC, PAST = 128, 512, 128
TILES = (SEQ // P, DEC // P)
PASSES = [(g, l) for l in range(DEPTH) for g in range(2)]
NT = [TILES[g] for g, _ in PASSES]
U0 = [sum(NT[:p]) for p in range(4)]
H, DK = 8, 64
QL, KVL, ROPE, DQ = 384, 256, 32, 96
SCALE = float(64 + 32) ** -0.5
NK, TOPK = 128, 16
EXPERTS = NK * NK
N_IN, N_OUT, N_WQ = 26, 8, 16
N_W = N_IN + N_OUT + N_WQ
N_ADA = 48
WR = 4
GR = 6
LEVELS = (4, 8, 16, 32, 64)
LV = len(LEVELS) + 2


def masks():
    s, t = np.arange(P)[:, None], np.arange(P)[None, :]
    out = np.zeros((2, 1 + len(LEVELS), P, P), np.int32)
    for d in range(2):
        a, b = (s, t) if d == 0 else (t, s)
        out[d, 0] = (s // 4 == t // 4) & (a <= b)
        for i, c in enumerate(LEVELS):
            out[d, 1 + i] = (s // (2 * c) == t // (2 * c)) & (a // c % 2 == 0) & (b // c % 2 == 1)
    return out


def build(nc, A, O):
    with ExitStack() as ctx:
        def sb(name, shape, dt=F32):
            return ctx.enter_context(nc.sbuf_tensor(name, shape, dt))

        def ps(name, shape):
            return ctx.enter_context(nc.psum_tensor(name, shape, F32))

        def sem(name):
            return ctx.enter_context(nc.semaphore(name))

        x = sb("x", [P, 5, D])
        gate = sb("gate", [P, D])
        hT = sb("hT", [P, KC, DEC])
        wring = sb("wring", [P, WR, KC, P])
        wqb = sb("wqb", [P, 3, H * DQ])
        keysT = wqb[:, :, :].rearrange("p a b -> p (a b)")[:, 0:2 * H * NK].rearrange("p (s k) -> p s k", k=NK)
        wkvb = sb("wkvb", [P, 2, H * P])
        U = sb("U", [P, 12288])
        sigq = U[:, 0:6144].rearrange("p (a t) -> p a t", t=DEC)
        Kt = U[:, 6144:6656].rearrange("p (g t) -> p g t", t=P)
        Pt = U[:, 6656:7168].rearrange("p (g t) -> p g t", t=P)
        Xt = U[:, 7168:7680].rearrange("p (g t) -> p g t", t=P)
        QP = U[:, 7680:8704].rearrange("p (b g t) -> p b g t", b=2, t=P)
        KX = U[:, 8704:9728].rearrange("p (b g t) -> p b g t", b=2, t=P)
        Asb = U[:, 9728:10752].rearrange("p (e g t) -> p e g t", e=2, t=P)
        KTn = U[:, 10752:11264].rearrange("p (g t) -> p g t", t=P)
        kT = U[:, 0:5120].rearrange("p (h k) -> p h k", h=H)
        vatt = U[:, 5120:7680].rearrange("p (a n) -> p a n", n=512)
        Pn = U[:, 7680:8960].rearrange("p (b k) -> p b k", b=2)
        PT = U[:, 8960:10240].rearrange("p (b a t) -> p b a t", b=2, t=P)
        qn = U[:, 10240:11008]
        QT = U[:, 11008:12032].rearrange("p (h t) -> p h t", t=P)
        cqT = hT[:, 0:3, :]
        ckvT = hT[:, 3:6, :].rearrange("p a b -> p (a b)")[:, 0:1280].rearrange("p (a b) -> p a b", a=2)
        qpT = U[:, 0:8192].rearrange("p (a t) -> p a t", t=DEC)
        SS = U[:, 8192:10240].rearrange("p (a k) -> p a k", k=NK)
        vg = sb("vg", [P, 2, 4, 512])
        V, GT = vg[:, 0], vg[:, 1]
        att = V
        h2 = vg[:, :, :, :].rearrange("p a b c -> p (a b c)").rearrange("p (t d) -> p t d", d=D)
        ring = sb("ring", [P, GR, D])
        rflat = ring[:, :, :].rearrange("p a b -> p (a b)")
        o = rflat[:, 0:2048].rearrange("p (t n) -> p t n", n=512)
        cq = rflat[:, 2048:3584].rearrange("p (t n) -> p t n", n=QL)
        ckv = rflat[:, 3584:4864].rearrange("p (t n) -> p t n", n=KVL)
        kpe = rflat[:, 4864:5024].rearrange("p (t n) -> p t n", n=ROPE)
        rt = rflat[:, 5024:5536].rearrange("p (i n) -> p i n", i=4)
        acc = sb("acc", [P, D])
        xn = sb("xn", [P, D])
        S = sb("S", [P, 2, 4, DK])
        ident = sb("ident", [P, P])
        mk = sb("mk", [P, 2, 6, P], I32)
        maskf = sb("maskf", [P, 2, P])
        rope = sb("rope", [P, 2, 4, 16])
        cond = sb("cond", [P, KC, 2])
        bada = sb("bada", [P, DEPTH, N_ADA])
        nrm = sb("nrm", [P, DEPTH, 2, KC])
        mods = sb("mods", [P, DEPTH, N_ADA, 2])
        Am = sb("Am", [P, DEPTH, 2, KC, 2])
        lbl = sb("lbl", [P, 2, DEPTH, 4])
        lb = sb("lb", [P, 2, DEPTH, 4])
        omlb = sb("omlb", [P, 2, DEPTH, 4])
        lt = sb("lt", [P, 4, 2, 4])
        qrow = sb("qrow", [P, DEPTH, QL])
        kvrow = sb("kvrow", [P, DEPTH, KVL])
        hrow = sb("hrow", [P, DEPTH, DK])
        frow = sb("frow", [P, D])
        st = sb("st", [P, 4])
        st8 = sb("st8", [P, 4, 32])
        mx = sb("mx", [P, 2, 1])
        nb = sb("nb", [P, 2, 1])
        es = sb("es", [P, H])
        ri = sb("ri", [P, H])
        v16 = sb("v16", [P, 2, TOPK])
        i16 = sb("i16", [P, 2, TOPK], U32)
        i16f = sb("i16f", [P, 2, TOPK])
        cand = sb("cand", [P, 2, TOPK * TOPK])
        pos = sb("pos", [P, TOPK], U32)
        ab = sb("ab", [P, 2, TOPK], U32)
        abf = sb("abf", [P, 2, TOPK])
        iota16 = sb("iota16", [P, TOPK])
        pick = sb("pick", [P, 2, TOPK])
        bs = sb("bs", [P, H, TOPK])
        gw = sb("gw", [P, H, TOPK])
        gs = sb("gs", [P, 2, H])
        eidx = sb("eidx", [P, 2, H * TOPK], I32)
        dot = sb("dot", [P, H * TOPK])
        gl = sb("gl", [P, H * TOPK])
        wv = sb("wv", [P, H * TOPK])

        pa = ps("pa", [P, 2, 512])
        tb = ps("tb", [P, 2, 512])
        pp = ps("pp", [P, 2, 1024])
        AE, AO = pp[:, 0, 0:512], pp[:, 0, 512:1024]
        OE, OO = pp[:, 1, 0:512], pp[:, 1, 512:1024]

        s_const = sem("s_const")
        s_cond = sem("s_cond")
        s_lbe = sem("s_lbe")
        s_lbd = sem("s_lbd")
        s_w = [sem(f"s_w{i}") for i in range(WR)]
        s_wused = sem("s_wused")
        s_ada = sem("s_ada")
        s_mods = sem("s_mods")
        s_sw = sem("s_sw")
        s_keys = sem("s_keys")
        s_ms = sem("s_ms")
        s_rt = sem("s_rt")
        s_xn = sem("s_xn")
        s_tp = sem("s_tp")
        s_te = sem("s_te")
        s_pj = sem("s_pj")
        s_pja = sem("s_pja")
        s_pjd = sem("s_pjd")
        s_lv = sem("s_lv")
        s_A = sem("s_A")
        s_Ac = sem("s_Ac")
        s_o = sem("s_o")
        s_oc = sem("s_oc")
        s_u = sem("s_u")
        s_S = sem("s_S")
        s_Sst = sem("s_Sst")
        s_hg = sem("s_hg")
        s_cn = sem("s_cn")
        s_pr = sem("s_pr")
        s_pra = sem("s_pra")
        s_qr = sem("s_qr")
        s_mx = sem("s_mx")
        s_pv = sem("s_pv")
        s_att = sem("s_att")
        s_tk = sem("s_tk")
        s_ge = sem("s_ge")
        s_bs = sem("s_bs")
        s_dot = sem("s_dot")
        s_gl = sem("s_gl")
        s_g = [sem(f"s_g{i}") for i in range(GR)]
        s_gused = sem("s_gused")
        s_y = sem("s_y")
        s_out = sem("s_out")
        c_dve = sem("c_dve")
        c_act = sem("c_act")
        s_io = sem("s_io")

        consts = [(ident[:, :], A["ident"]), (mk[:, :, :, :], A["masks"]), (maskf[:, :, :], A["maskf"]),
                  (rope[:, :, :, :], A["rope"]), (cond[:, :, :], A["cond"]), (bada[:, :, :], A["b_ada"]),
                  (nrm[:, :, :, :], A["nrm"]), (lbl[:, :, :, :], A["lbl"]), (x[:, :, :], A["x"]),
                  (qrow[:, :, :], A["qrow"]), (kvrow[:, :, :], A["kvrow"]), (hrow[:, :, :], A["hrow"]),
                  (frow[:, :], A["frow"])]
        CONST = 16 * len(consts)

        block = ctx.enter_context(nc.Block())

        def freed(n):
            p, m = divmod(n, N_W)
            if N_IN <= m < N_IN + N_OUT:
                return s_pjd, p * N_OUT + m - N_IN + 1
            return s_pja, p * (N_IN + N_WQ) + (m if m < N_IN else m - N_OUT) + 1

        def has_ctx(p):
            return PASSES[p][0]

        def n_small(p):
            return sum(2 + 3 * has_ctx(i) for i in range(p + 1))

        class Count:
            def __init__(self):
                self.n = 0

            def next(self):
                self.n += 1
                return self.n - 1

        @block.sync
        def _(sp):
            for dst, src in consts:
                sp.dma_start(dst, src).then_inc(s_const, 16)
            w = Count()

            def weight(src):
                n = w.next()
                if n >= WR:
                    sp.wait_ge(s_wused, n - WR + 1)
                if src.shape[2] == P:
                    dst = wring[:, n % WR, :, :]
                else:
                    dst = wring[:, n % WR, :, 0:src.shape[2]]
                sp.dma_start(dst, src).then_inc(s_w[n % WR], 16)

            for l in range(DEPTH):
                for j in range(N_ADA):
                    weight(A["w_ada"][l, j])
            for p, (g, l) in enumerate(PASSES):
                if p:
                    sp.wait_ge(s_S, 4 * U0[p])
                    sp.wait_ge(s_tk, U0[p])
                    sp.wait_ge(s_gused, 256 * U0[p])
                sp.dma_start(wqb[:, :, :], A["wqb"][l]).then_inc(s_sw, 16)
                sp.dma_start(wkvb[:, :, :], A["wkvb"][l]).then_inc(s_sw, 16)
                if g:
                    sp.dma_start(ckv[:, 0, :], A["cache_ckv"][l]).then_inc(s_sw, 16)
                    sp.dma_start(kpe[:, 0, :], A["cache_kpe"][l]).then_inc(s_sw, 16)
                    sp.wait_ge(s_Sst, 16 * (l + 1))
                    sp.dma_start(S[:, :, :, :], A["state"][l]).then_inc(s_sw, 16)
                for j in range(N_IN - 1):
                    weight(A["w_in"][l, j])
                weight(A["w_in_tail"][l])
                if not g:
                    sp.wait_ge(s_cn, 2 * p + 2)
                    sp.dma_start(O["ckv"][l], ckv[:, 0, :]).then_inc(s_out, 16)
                    sp.dma_start(O["kpe"][l], kpe[:, 0, :]).then_inc(s_out, 16)
                    sp.wait_ge(s_S, 4 * (U0[p] + NT[p]))
                    sp.dma_start(O["state"][l], S[:, :, :, :]).then_inc(s_Sst, 16)
                for j in range(N_OUT):
                    weight(A["w_out"][l, j])
                sp.wait_ge(s_att, U0[p] + NT[p])
                sp.dma_start(keysT, A["keys"][l]).then_inc(s_keys, 16)
                for j in range(N_WQ):
                    weight(A["w_q"][l, j])
                if l == DEPTH - 1:
                    for t in range(NT[p]):
                        n = sum(NT[q] for q in range(2, p)) + t
                        sp.wait_ge(s_y, 2 * n + 1)
                        sp.dma_start(O["y"][(0, 1)[g] + t], xn[:, :]).then_inc(s_io, 16)
            sp.wait_ge(s_out, 16 * 4)
            sp.wait_ge(s_Sst, 16 * 2)
            sp.wait_ge(s_io, 16 * 5)

        @block.gpsimd
        def _(pool):
            pool.iota(iota16[:, :], [[1, TOPK]], base=0, channel_multiplier=0,
                      allow_small_or_imprecise_dtypes=True).then_inc(s_const, 16)
            n = 0
            for p, (g, l) in enumerate(PASSES):
                for t in range(NT[p]):
                    u = U0[p] + t
                    pool.wait_ge(s_tk, u + 1)
                    for table in ("peer_u", "peer_v"):
                        for k in range(H * TOPK):
                            if n >= GR:
                                pool.wait_ge(s_gused, n - GR + 1)
                            pool.indirect_dma_start(
                                ring[:, n % GR, :], None, A[table],
                                bass.IndirectOffsetOnAxis(ap=eidx[:, u % 2, k:k + 1], axis=0),
                            ).then_inc(s_g[n % GR], 16)
                            n += 1

        @block.tensor
        def _(pe):
            w, tr, pr, pj = Count(), Count(), Count(), Count()

            def wtile():
                n = w.next()
                pe.wait_ge(s_w[n % WR], 16 * (n // WR + 1))
                return wring[:, n % WR]

            def transposes(pieces, width=P):
                n = tr.next()
                if n >= 2:
                    pe.wait_ge(s_te, n - 1)
                for i, piece in enumerate(pieces):
                    m = piece.shape[1]
                    ins = nc.tensor.transpose(tb[0:m, n % 2, i * P:(i + 1) * P], piece, ident[:, :])
                ins.then_inc(s_tp, 1)

            def pair():
                n = pr.next()
                if n >= 2:
                    pe.wait_ge(s_pra, n - 1)
                return pp[:, n % 2, :]

            def bank():
                n = pj.next()
                if n >= 2:
                    pe.wait_ge(*freed(n - 2))
                return pa[:, n % 2, :]

            def gate_row(p, which):
                g, l = PASSES[p]
                b = pair()
                for c in range(KC):
                    col = mods[:, l, (2 + 3 * which) * KC + c, g:g + 1]
                    ins = nc.tensor.matmul(b[:, c * P:(c + 1) * P], col.to_broadcast([P, P]), ident[:, :],
                                           start=True, stop=True)
                ins.then_inc(s_pr, 1)

            pe.wait_ge(s_const, CONST + 16)
            pe.wait_ge(s_cond, 1)
            for l in range(DEPTH):
                for j in range(N_ADA):
                    wt = wtile()
                    for c in range(KC):
                        ins = nc.tensor.matmul(pa[:, l, 2 * j:2 * j + 2], wt[:, c, :], cond[:, c, :],
                                               start=(c == 0), stop=(c == KC - 1))
                    ins.then_inc(s_wused, 1)
                pe.wait_ge(s_wused, (l + 1) * N_ADA)
                pe.sem_inc(s_ada, 1)
            pe.wait_ge(s_mods, 2)

            for p, (g, l) in enumerate(PASSES):
                nt, u0, T = NT[p], U0[p], NT[p] * P
                kt_n = nt + g
                for t in range(nt):
                    pe.wait_ge(s_xn, 2 * u0 + t + 1)
                    for i in range(2):
                        transposes([xn[:, (4 * i + c) * P:(4 * i + c + 1) * P] for c in range(4)])
                pe.wait_ge(s_te, tr.n)
                for j in range(N_IN):
                    wt = wtile()
                    b = bank()
                    if j < 12:
                        for c in range(KC):
                            ins = nc.tensor.matmul(b[:, 0:T], wt[:, c, :], hT[:, c, 0:T],
                                                   start=(c == 0), stop=(c == KC - 1))
                    else:
                        m = P if j < N_IN - 1 else ROPE
                        for t in range(nt):
                            for c in range(KC):
                                ins = nc.tensor.matmul(b[:, t * P:t * P + m], hT[:, c, t * P:(t + 1) * P],
                                                       wt[:, c, 0:m], start=(c == 0), stop=(c == KC - 1))
                    ins.then_inc(s_pj, 1)
                    pe.wait_ge(s_pj, pj.n)
                    pe.sem_inc(s_wused, 1)
                pe.wait_ge(s_pja, freed(pj.n - 1)[1])
                if g:
                    pe.wait_ge(s_sw, 16 * n_small(p))
                pe.wait_ge(s_pra, pr.n)
                for d in range(2):
                    for i in range(nt):
                        hu = 2 * u0 + d * nt + i
                        t = i if d == 0 else nt - 1 - i
                        for m in range(LV):
                            li = hu * LV + m
                            pe.wait_ge(s_lv, li + 1)
                            if m < LV - 1:
                                if m or hu:
                                    pe.wait_ge(s_Ac, hu * (LV - 1) + m)
                                for gg in range(4):
                                    for e, dst in ((0, AE), (1, AO)):
                                        r = slice(64 * e, 64 * e + 64)
                                        ins = nc.tensor.matmul(dst[:, gg * P:(gg + 1) * P], KX[r, li % 2, gg, :],
                                                               QP[r, li % 2, gg, :], start=True, stop=True)
                                ins.then_inc(s_A, 1)
                            else:
                                transposes([KX[:, li % 2, gg, :] for gg in range(4)])
                                if hu:
                                    pe.wait_ge(s_oc, hu)
                                pe.wait_ge(s_Ac, (hu + 1) * (LV - 1))
                                pe.wait_ge(s_S, 2 * hu + 1)
                                for gg in range(4):
                                    for e, dst in ((0, OE), (1, OO)):
                                        hh = 2 * gg + e
                                        r = slice(64 * e, 64 * e + 64)
                                        out = dst[:, gg * DK:(gg + 1) * DK]
                                        nc.tensor.matmul(out, Asb[:, e, gg, :], V[:, t, hh * DK:(hh + 1) * DK],
                                                         start=True, stop=False)
                                        ins = nc.tensor.matmul(out, QP[r, li % 2, gg, :], S[r, d, gg, :],
                                                               start=False, stop=True)
                                ins.then_inc(s_o, 1)
                                pe.wait_ge(s_te, tr.n)
                                if hu:
                                    pe.wait_ge(s_S, 2 * hu)
                                for gg in range(4):
                                    ins = nc.tensor.matmul(pa[:, 0, gg * P:(gg + 1) * P], KTn[:, gg, :],
                                                           V[:, t, gg * P:(gg + 1) * P], start=True, stop=True)
                                ins.then_inc(s_u, 1)
                pe.wait_ge(s_cn, 2 * p + 2)
                pe.wait_ge(s_sw, 16 * n_small(p))
                for t in range(nt):
                    transposes([cq[:, t, i * P:(i + 1) * P] for i in range(3)])
                for t in range(kt_n):
                    transposes([ckv[:, t, i * P:(i + 1) * P] for i in range(2)] + [kpe[:, t, :]])
                pe.wait_ge(s_te, tr.n)
                pe.wait_ge(s_oc, 2 * (u0 + nt))
                keys = kt_n * P
                for hh in range(H):
                    b = pair()
                    for k0 in range(0, keys, 512):
                        kn = min(512, keys - k0)
                        for c in range(2):
                            ins = nc.tensor.matmul(b[0:64, k0:k0 + kn], wkvb[:, c, hh * P:hh * P + 64],
                                                   ckvT[:, c, k0:k0 + kn], start=(c == 0), stop=(c == 1))
                    ins.then_inc(s_pr, 1)
                wv4 = wkvb[:, :, :].rearrange("p c (h n) -> p c h n", h=H)
                for t in range(kt_n):
                    b = pair()
                    for c in range(2):
                        ins = nc.tensor.matmul(b[:, 0:512].rearrange("p (h n) -> p h n", h=H),
                                               ckvT[:, c, t * P:(t + 1) * P], wv4[:, c, :, 64:128],
                                               start=(c == 0), stop=(c == 1))
                    ins.then_inc(s_pr, 1)
                for t in range(nt):
                    b = pair()
                    for half in range(2):
                        for c in range(3):
                            ins = nc.tensor.matmul(b[:, half * 512:half * 512 + QL], cqT[:, c, t * P:(t + 1) * P],
                                                   wqb[:, c, half * QL:(half + 1) * QL], start=(c == 0), stop=(c == 2))
                    ins.then_inc(s_pr, 1)
                    if g:
                        pe.wait_ge(s_qr, 4 * l + t + 1)
                    else:
                        pe.wait_ge(s_pra, pr.n)
                    for i in range(2):
                        transposes([qn[:, (4 * i + c) * DQ:(4 * i + c + 1) * DQ] for c in range(4)])
                    pe.wait_ge(s_te, tr.n)
                    if t >= 2 or (t < 2 and p):
                        pe.wait_ge(s_att, u0 + t - 1 if t >= 1 else u0)
                    else:
                        pe.wait_ge(s_S, 4 * (u0 + nt))

                    def scores(hh):
                        b = pair()
                        for k0 in range(0, keys, 512):
                            kn = min(512, keys - k0)
                            ins = nc.tensor.matmul(b[:, k0:k0 + kn], QT[0:DQ, hh, :], kT[0:DQ, hh, k0:k0 + kn],
                                                   start=True, stop=True)
                        ins.then_inc(s_pr, 1)

                    scores(0)
                    for hh in range(H):
                        if hh + 1 < H:
                            scores(hh + 1)
                        pe.wait_ge(s_pra, pr.n - (1 if hh + 1 < H else 0))
                        hi = hh % 2
                        transposes([Pn[:, hi, a * P:(a + 1) * P] for a in range(min(4, kt_n))])
                        if kt_n > 4:
                            transposes([Pn[:, hi, 4 * P:5 * P]])
                        pe.wait_ge(s_te, tr.n)
                        for a in range(kt_n):
                            ins = nc.tensor.matmul(pa[:, t % 2, hh * DK:(hh + 1) * DK], PT[:, hi, a, :],
                                                   vatt[:, a, hh * DK:(hh + 1) * DK], start=(a == 0), stop=(a == kt_n - 1))
                    ins.then_inc(s_pv, 1)
                gate_row(p, 0)
                pe.wait_ge(s_hg, p + 1)
                for t in range(nt):
                    transposes([o[:, t, c * P:(c + 1) * P] for c in range(4)])
                pe.wait_ge(s_att, u0 + nt)
                for t in range(nt):
                    transposes([att[:, t, c * P:(c + 1) * P] for c in range(4)])
                pe.wait_ge(s_te, tr.n)
                for j in range(N_OUT):
                    wt = wtile()
                    b = bank()
                    for t in range(nt):
                        for c in range(KC):
                            ins = nc.tensor.matmul(b[:, t * P:(t + 1) * P], hT[:, c, t * P:(t + 1) * P], wt[:, c, :],
                                                   start=(c == 0), stop=(c == KC - 1))
                    ins.then_inc(s_pj, 1)
                    pe.wait_ge(s_pj, pj.n)
                    pe.sem_inc(s_wused, 1)
                for t in range(nt):
                    pe.wait_ge(s_xn, 2 * u0 + nt + t + 1)
                    for i in range(2):
                        transposes([xn[:, (4 * i + c) * P:(4 * i + c + 1) * P] for c in range(4)])
                    pe.wait_ge(s_te, tr.n)
                    for i in range(2):
                        transposes([hT[:, 4 * i + c, t * P:(t + 1) * P] for c in range(4)])
                pe.wait_ge(s_pjd, (p + 1) * N_OUT)
                gate_row(p, 1)
                for j in range(N_WQ):
                    wt = wtile()
                    b = bank()
                    for c in range(KC):
                        ins = nc.tensor.matmul(b[:, 0:T], wt[:, c, :], hT[:, c, 0:T], start=(c == 0), stop=(c == KC - 1))
                    ins.then_inc(s_pj, 1)
                    pe.wait_ge(s_pj, pj.n)
                    pe.sem_inc(s_wused, 1)
                pe.wait_ge(s_pja, freed(pj.n - 1)[1])
                pe.wait_ge(s_keys, 16 * (p + 1))
                for t in range(nt):
                    for i in range(2):
                        b = pair()
                        for a in range(8):
                            n = 8 * i + a
                            ins = nc.tensor.matmul(b[:, a * P:(a + 1) * P], qpT[:, n, t * P:(t + 1) * P], keysT[:, n, :],
                                                   start=True, stop=True)
                        ins.then_inc(s_pr, 1)

        @block.scalar
        def _(act):
            chain, tr, pr, pj = Count(), Count(), Count(), Count()

            def got_t():
                n = tr.next()
                act.wait_ge(s_tp, n + 1)
                return tb[:, n % 2, :].rearrange("p (c t) -> p c t", t=P)

            def got_pair():
                n = pr.next()
                act.wait_ge(s_pr, n + 1)
                return pp[:, n % 2, :]

            def copy(dst, src, **kw):
                return nc.scalar.activation(dst, src, ACT.Copy, **kw)

            def root():
                nonlocal roots
                act.wait_ge(s_ms, roots + 1)
                roots += 1

            def modulated(p, which, t):
                g, l = PASSES[p]
                for i in range(2):
                    src = got_t()
                    for c in range(4):
                        k = 4 * i + c
                        ins = nc.scalar.activation(hT[:, k, t * P:(t + 1) * P], src[:, c, :], ACT.Identity,
                                                   scale=Am[:, l, which, k, g:g + 1],
                                                   bias=mods[:, l, 3 * which * KC + k, g:g + 1])
                    ins.then_inc(s_te, 1)

            roots = 0
            act.wait_ge(s_const, CONST + 16)
            nc.scalar.activation(cond[:, :, :], cond[:, :, :], ACT.Silu).then_inc(s_cond, 1)
            act.wait_ge(s_lbd, 1)
            nc.scalar.activation(lt[:, 0:2, :, :], lt[:, 0:2, :, :], ACT.Exp).then_inc(s_lbe, 1)
            act.wait_ge(s_mods, 2)

            for p, (g, l) in enumerate(PASSES):
                nt, u0, T = NT[p], U0[p], NT[p] * P
                kt_n = nt + g
                for t in range(nt):
                    root()
                    nc.scalar.activation(st[:, 2:3], st[:, 1:2], ACT.Sqrt).then_inc(s_rt, 1)
                    modulated(p, 0, t)
                for j in range(N_IN):
                    n = pj.next()
                    act.wait_ge(s_pj, p * N_W + j + 1)
                    b = pa[:, (p * N_W + j) % 2, :]
                    nat = b.rearrange("p (t n) -> p t n", n=P)[:, 0:nt, :]
                    if j < 4:
                        ins = copy(sigq[:, j, 0:T], b[:, 0:T], scale=DK ** -0.5)
                    elif j < 12:
                        ins = nc.scalar.activation(sigq[:, j, 0:T], b[:, 0:T], ACT.Sigmoid)
                    elif j < 16:
                        ins = copy(V[:, 0:nt, (j - 12) * P:(j - 11) * P], nat)
                    elif j < 20:
                        ins = nc.scalar.activation(GT[:, 0:nt, (j - 16) * P:(j - 15) * P], nat, ACT.Silu)
                    elif j < 23:
                        ins = copy(cq[:, 0:nt, (j - 20) * P:(j - 19) * P], nat)
                    elif j < 25:
                        ins = copy(ckv[:, g:g + nt, (j - 23) * P:(j - 22) * P], nat)
                    else:
                        ins = copy(kpe[:, g:g + nt, :], nat[:, :, 0:ROPE])
                    ins.then_inc(s_pja, 1)
                for d in range(2):
                    for i in range(nt):
                        hu = 2 * u0 + d * nt + i
                        src = got_t()
                        if hu:
                            act.wait_ge(s_u, hu)
                        copy(KTn[:, :, :], src).then_inc(s_te, 1)
                root()
                nc.scalar.activation(st8[:, 2, 0:8 * nt], st8[:, 1, 0:8 * nt], ACT.Sqrt).then_inc(s_rt, 1)
                root()
                nc.scalar.activation(st8[:, 2, 0:8], st8[:, 1, 0:8], ACT.Sqrt).then_inc(s_rt, 1)
                for t in range(nt):
                    src = got_t()
                    copy(cqT[:, :, t * P:(t + 1) * P], src[:, 0:3, :]).then_inc(s_te, 1)
                for t in range(kt_n):
                    src = got_t()
                    copy(ckvT[:, :, t * P:(t + 1) * P], src[:, 0:2, :])
                    copy(kT[64:96, :, t * P:(t + 1) * P],
                         src[0:ROPE, 2:3, :].to_broadcast([ROPE, H, P])).then_inc(s_te, 1)
                keys = kt_n * P
                for hh in range(H):
                    b = got_pair()
                    copy(kT[0:64, hh, 0:keys], b[0:64, 0:keys]).then_inc(s_pra, 1)
                for t in range(kt_n):
                    b = got_pair()
                    copy(vatt[:, t, :], b[:, 0:512]).then_inc(s_pra, 1)
                for t in range(nt):
                    b = got_pair()
                    copy(qn.rearrange("p (a n) -> p a n", a=2), b.rearrange("p (a n) -> p a n", a=2)[:, :, 0:QL])\
                        .then_inc(s_pra, 1)
                    for i in range(2):
                        src = got_t()
                        copy(QT[0:DQ, 4 * i:4 * i + 4, :], src[0:DQ, :, :]).then_inc(s_te, 1)
                    if t or p:
                        act.wait_ge(s_att, u0 + t)
                    for hh in range(H):
                        b = got_pair()
                        act.wait_ge(s_mx, 8 * (u0 + t) + hh + 1)
                        nc.scalar.activation(Pn[:, hh % 2, 0:keys], b[:, 0:keys], ACT.Exp, scale=SCALE,
                                             bias=nb[:, hh % 2, :], accum_out=es[:, hh:hh + 1]).then_inc(s_pra, 1)
                        src = got_t()
                        a = min(4, kt_n)
                        copy(PT[:, hh % 2, 0:a, :], src[:, 0:a, :]).then_inc(s_te, 1)
                        if kt_n > 4:
                            src = got_t()
                            copy(PT[:, hh % 2, 4, :], src[:, 0, :]).then_inc(s_te, 1)
                b = got_pair()
                copy(gate[:, :], b).then_inc(s_pra, 1)
                for half in range(2):
                    for t in range(nt):
                        src = got_t()
                        copy(hT[:, 4 * half:4 * half + 4, t * P:(t + 1) * P], src).then_inc(s_te, 1)
                for t in range(nt):
                    root()
                    nc.scalar.activation(st[:, 2:3], st[:, 1:2], ACT.Sqrt).then_inc(s_rt, 1)
                    modulated(p, 1, t)
                    for i in range(2):
                        src = got_t()
                        copy(h2[:, t, 512 * i:512 * (i + 1)].rearrange("p (c t) -> p c t", t=P), src).then_inc(s_te, 1)
                b = got_pair()
                copy(gate[:, :], b).then_inc(s_pra, 1)
                for j in range(N_WQ):
                    n = p * N_W + N_IN + N_OUT + j
                    act.wait_ge(s_pj, n + 1)
                    copy(qpT[:, j, 0:T], pa[:, n % 2, 0:T]).then_inc(s_pja, 1)
                for t in range(nt):
                    u = u0 + t
                    if t == 0:
                        for i in range(2):
                            b = got_pair()
                            copy(SS[:, 8 * i:8 * i + 8, :], b.rearrange("p (a k) -> p a k", k=NK)).then_inc(s_pra, 1)
                    act.wait_ge(s_bs, u + 1)
                    nc.scalar.activation(gw[:, :, :], bs[:, :, :], ACT.Exp).then_inc(s_ge, 1)
                    if t + 1 < nt:
                        act.wait_ge(s_tk, u + 1)
                        for i in range(2):
                            b = got_pair()
                            copy(SS[:, 8 * i:8 * i + 8, :], b.rearrange("p (a k) -> p a k", k=NK)).then_inc(s_pra, 1)
                    act.wait_ge(s_dot, u + 1)
                    nc.scalar.activation(gl[:, :], dot[:, :], ACT.Gelu).then_inc(s_gl, 1)
                if l == DEPTH - 1:
                    for t in range(nt):
                        root()
                        nc.scalar.activation(st[:, 2:3], st[:, 1:2], ACT.Sqrt).then_inc(s_rt, 1)

        @block.vector
        def _(dve):
            count, pr, roots = Count(), Count(), Count()
            v = nc.vector

            def link(ins):
                count.n += 1
                ins.then_inc(c_dve, 1)
                dve.wait_ge(c_dve, count.n)

            def norm(src, out_scale_row=None):
                link(v.tensor_tensor_reduce(xn[:, :], src, src, 1.0, 0.0, ALU.mult, ALU.add, st[:, 0:1]))
                v.tensor_scalar(st[:, 1:2], st[:, 0:1], 1.0 / D, EPS, ALU.mult, ALU.add).then_inc(s_ms, 1)
                dve.wait_ge(s_rt, roots.next() + 1)
                link(v.reciprocal(st[:, 3:4], st[:, 2:3]))
                if out_scale_row is None:
                    v.tensor_scalar(xn[:, :], src, st[:, 3:4], None, ALU.mult).then_inc(s_xn, 1)
                else:
                    v.scalar_tensor_tensor(xn[:, :], src, st[:, 3:4], out_scale_row, ALU.mult, ALU.mult)\
                        .then_inc(s_y, 1)

            dve.wait_ge(s_const, CONST + 16)
            top = lt[:, 2]
            link(v.tensor_tensor(top, lbl[:, :, 0, :], lbl[:, :, 1, :], ALU.max))
            for i in range(DEPTH):
                ins = v.tensor_tensor(lt[:, i], lbl[:, :, i, :], top, ALU.subtract)
                if i == 0:
                    link(ins)
            ins.then_inc(s_lbd, 1)
            dve.wait_ge(s_lbe, 1)
            link(v.tensor_tensor(lt[:, 3], lt[:, 0], lt[:, 1], ALU.add))
            link(v.reciprocal(lt[:, 3], lt[:, 3]))
            link(v.tensor_tensor(lt[:, 0], lt[:, 0], lt[:, 3], ALU.mult))
            link(v.tensor_tensor(lt[:, 1], lt[:, 1], lt[:, 3], ALU.mult))
            link(v.tensor_tensor(lb[:, :, 0, :], lt[:, 0], lt[:, 0], ALU.subtract))
            link(v.tensor_tensor(lt[:, 2], lt[:, 0], lt[:, 1], ALU.add))
            link(v.tensor_tensor(lb[:, :, 1, :], lt[:, 2], lt[:, 0], ALU.subtract))
            link(v.tensor_scalar(omlb[:, :, :, :], lb[:, :, :, :], -1.0, 1.0, ALU.mult, ALU.add))
            for l in range(DEPTH):
                dve.wait_ge(s_ada, l + 1)
                link(v.tensor_tensor(mods[:, l, :, :], pa[:, l, 0:2 * N_ADA].rearrange("p (j c) -> p j c", c=2),
                                     bada[:, l, :].unsqueeze(2).to_broadcast([P, N_ADA, 2]), ALU.add))
                for which in range(2):
                    a = Am[:, l, which, :, :]
                    link(v.tensor_scalar(a, mods[:, l, (3 * which + 1) * KC:(3 * which + 2) * KC, :], 1.0, None, ALU.add))
                    ins = v.tensor_tensor(a, a, nrm[:, l, which, :].unsqueeze(2).to_broadcast([P, KC, 2]), ALU.mult)
                    if which == 0:
                        link(ins)
                ins.then_inc(s_mods, 1)

            gn = 0
            for p, (g, l) in enumerate(PASSES):
                nt, u0, T = NT[p], U0[p], NT[p] * P
                kt_n = nt + g
                keys = kt_n * P
                xs = x[:, g:g + nt, :]
                trn = tr_before(p)
                if p == 3:
                    dve.wait_ge(s_io, 16)
                for t in range(nt):
                    if t:
                        dve.wait_ge(s_tp, trn + 2 * t)
                    norm(xs[:, t, :])
                if not g:
                    if p:
                        dve.wait_ge(s_Sst, 16 * l)
                    link(v.memset(S[:, :, :, :], 0.0))
                else:
                    dve.wait_ge(s_sw, 16 * n_small(p))
                dve.wait_ge(s_pja, freed(p * N_W + N_IN - 1)[1])
                for d in range(2):
                    for a in range(4):
                        f = sigq[:, 4 + 4 * d + a, 0:T]
                        link(v.tensor_scalar(f, f, omlb[:, d, l, a:a + 1], lb[:, d, l, a:a + 1], ALU.mult, ALU.add))
                f = sigq[:, 4:12, 0:T]
                link(v.tensor_scalar(f, f, FLOOR, None, ALU.max))
                for d in range(2):
                    for i in range(nt):
                        hu = 2 * u0 + d * nt + i
                        t = i if d == 0 else nt - 1 - i
                        cols = slice(t * P, (t + 1) * P)
                        qt, ft = sigq[:, 0:4, cols], sigq[:, 4 + 4 * d:8 + 4 * d, cols]
                        link(v.tensor_scalar(Kt[:, :, :], ft, -1.0, 1.0, ALU.mult, ALU.add))
                        link(v.tensor_copy(Pt[:, :, :], ft))
                        link(v.memset(Xt[:, :, :], 1.0))

                        def double(c):
                            hi, lo = (1, 0) if d == 0 else (0, 1)
                            e = c - 1 if d == 0 else 0
                            pv = Pt[:, :, :].rearrange("p g (n two c) -> p (g n) two c", two=2, c=c)
                            xv = Xt[:, :, :].rearrange("p g (n two c) -> p (g n) two c", two=2, c=c)
                            m = 4 * P // (2 * c)
                            link(v.tensor_tensor(xv[:, :, lo, :], xv[:, :, lo, :],
                                                 pv[:, :, hi, e:e + 1].to_broadcast([P, m, c]), ALU.mult))
                            link(v.tensor_tensor(pv[:, :, hi, :], pv[:, :, hi, :],
                                                 pv[:, :, lo, e:e + 1].to_broadcast([P, m, c]), ALU.mult))

                        def operands(m):
                            li = hu * LV + m
                            if li >= 2:
                                a, b = divmod(li - 2, LV)
                                if b < LV - 1:
                                    dve.wait_ge(s_A, a * (LV - 1) + b + 1)
                                else:
                                    dve.wait_ge(s_o, a + 1)
                                    dve.wait_ge(s_tp, tr_hg(a) + 1)
                            if m == 0:
                                link(v.reciprocal(KX[:, li % 2], Pt[:, :, :]))
                                link(v.tensor_tensor(KX[:, li % 2], KX[:, li % 2], Kt[:, :, :], ALU.mult))
                            else:
                                link(v.tensor_tensor(KX[:, li % 2], Xt[:, :, :], Kt[:, :, :], ALU.mult))
                            v.tensor_tensor(QP[:, li % 2], Pt[:, :, :], qt, ALU.mult).then_inc(s_lv, 1)

                        def merge(m):
                            dve.wait_ge(s_A, hu * (LV - 1) + m + 1)
                            if m == 0 and hu:
                                dve.wait_ge(s_o, hu)
                            for e, src in ((0, AE), (1, AO)):
                                src = src.rearrange("p (g t) -> p g t", t=P)
                                if m == 0:
                                    ins = v.tensor_tensor(Asb[:, e], src, maskf[:, d, :].unsqueeze(1).to_broadcast([P, 4, P]),
                                                          ALU.mult)
                                else:
                                    ins = v.copy_predicated(Asb[:, e], mk[:, d, m, :].unsqueeze(1).to_broadcast([P, 4, P]), src)
                                if e == 0:
                                    link(ins)
                            ins.then_inc(s_Ac, 1)
                            dve.wait_ge(s_Ac, hu * (LV - 1) + m + 1)

                        double(1)
                        double(2)
                        operands(0)
                        for m, c in enumerate(LEVELS):
                            operands(m + 1)
                            dve.wait_ge(s_lv, hu * LV + m + 2)
                            merge(m)
                            double(c)
                        dve.sem_inc(s_S, 1)
                        operands(LV - 1)
                        merge(LV - 2)
                        dve.wait_ge(s_o, hu + 1)
                        ov = o[:, t, :].rearrange("p (g e n) -> p g e n", e=2, n=DK)
                        for e, src in ((0, OE), (1, OO)):
                            src = src[:, 0:4 * DK].rearrange("p (g n) -> p g n", n=DK)
                            if d == 0:
                                ins = v.tensor_copy(ov[:, :, e, :], src)
                            else:
                                ins = v.tensor_tensor(ov[:, :, e, :], src, ov[:, :, e, :], ALU.add)
                            if e == 0:
                                link(ins)
                        ins.then_inc(s_oc, 1)
                        e = P - 1 if d == 0 else 0
                        link(v.tensor_tensor(S[:, d], S[:, d], Pt[:, :, e:e + 1].to_broadcast([P, 4, DK]), ALU.mult))
                        dve.wait_ge(s_u, hu + 1)
                        uv = pa[:, 0, :].rearrange("p (g n) -> p g n", n=P)
                        link(v.tensor_tensor(S[0:64, d], uv[0:64, :, 0:64], S[0:64, d], ALU.add))
                        v.tensor_tensor(S[64:128, d], uv[64:128, :, 64:128], S[64:128, d], ALU.add).then_inc(s_S, 1)
                        dve.wait_ge(s_S, 2 * (hu + 1))
                dve.wait_ge(s_oc, 2 * (u0 + nt))
                ov = o[:, 0:nt, :].rearrange("p t (h n) -> p (t h) n", n=DK)
                sq = U[:, 0:512 * nt].rearrange("p (a n) -> p a n", n=DK)
                link(v.tensor_tensor(sq, ov, ov, ALU.mult))
                link(v.tensor_reduce(st8[:, 0, 0:8 * nt], sq, AX.X, ALU.add))
                v.tensor_scalar(st8[:, 1, 0:8 * nt], st8[:, 0, 0:8 * nt], 1.0 / DK, EPS, ALU.mult, ALU.add).then_inc(s_ms, 1)
                dve.wait_ge(s_rt, roots.next() + 1)
                link(v.reciprocal(st8[:, 3, 0:8 * nt], st8[:, 2, 0:8 * nt]))
                link(v.tensor_tensor(ov, ov, st8[:, 3, 0:8 * nt].unsqueeze(2).to_broadcast([P, 8 * nt, DK]), ALU.mult))
                link(v.tensor_tensor(ov, ov, hrow[:, l, :].unsqueeze(1).to_broadcast([P, 8 * nt, DK]), ALU.mult))
                v.tensor_tensor(o[:, 0:nt, :], o[:, 0:nt, :], GT[:, 0:nt, :], ALU.mult).then_inc(s_hg, 1)
                link(v.memset(st8[:, 0, 0:8], 1.0))
                for t in range(nt):
                    link(v.tensor_tensor_reduce(xn[:, 0:QL], cq[:, t, :], cq[:, t, :], 1.0 / QL, EPS, ALU.mult, ALU.add,
                                                st8[:, 0, t:t + 1]))
                    link(v.tensor_tensor_reduce(xn[:, 0:KVL], ckv[:, g + t, :], ckv[:, g + t, :], 1.0 / KVL, EPS, ALU.mult,
                                                ALU.add, st8[:, 0, 4 + t:5 + t]))
                v.tensor_copy(st8[:, 1, 0:8], st8[:, 0, 0:8]).then_inc(s_ms, 1)
                dve.wait_ge(s_rt, roots.next() + 1)
                link(v.reciprocal(st8[:, 3, 0:8], st8[:, 2, 0:8]))
                for t in range(nt):
                    link(v.scalar_tensor_tensor(cq[:, t, :], cq[:, t, :], st8[:, 3, t:t + 1], qrow[:, l, :],
                                                ALU.mult, ALU.mult))
                    ins = v.scalar_tensor_tensor(ckv[:, g + t, :], ckv[:, g + t, :], st8[:, 3, 4 + t:5 + t], kvrow[:, l, :],
                                                 ALU.mult, ALU.mult)
                    if t + 1 < nt:
                        link(ins)
                ins.then_inc(s_cn, 1)

                def rotate(vec, shape, cos, sin):
                    x1, x2 = vec[:, :, 0, :], vec[:, :, 1, :]
                    n = shape
                    tmp = [rt[:, i, 0:n * 8].rearrange("p (a b) -> p a b", b=8) for i in range(4)]
                    link(v.tensor_tensor(tmp[0], x1, cos, ALU.mult))
                    link(v.tensor_tensor(tmp[1], x2, sin, ALU.mult))
                    link(v.tensor_tensor(tmp[2], x1, sin, ALU.mult))
                    link(v.tensor_tensor(tmp[3], x2, cos, ALU.mult))
                    link(v.tensor_tensor(x1, tmp[0], tmp[1], ALU.subtract))
                    return v.tensor_tensor(x2, tmp[2], tmp[3], ALU.add)

                if g:
                    for a in range(4):
                        vec = kpe[:, 1 + a, :].rearrange("p (x two n) -> p x two n", x=2, two=2)
                        ins = rotate(vec, 2, rope[:, 0, a, :].rearrange("p (x n) -> p x n", x=2),
                                     rope[:, 1, a, :].rearrange("p (x n) -> p x n", x=2))
                        if a < 3:
                            link(ins)
                    ins.then_inc(s_cn, 1)
                else:
                    dve.wait_ge(s_cn, 2 * p + 1)
                    dve.sem_inc(s_cn, 1)
                prn = pr_before(p) + 8 + kt_n
                for t in range(nt):
                    u = u0 + t
                    prn += 1
                    if g:
                        dve.wait_ge(s_pra, prn)
                        qv = qn.rearrange("p (h n) -> p h n", n=DQ)
                        for ax in range(2):
                            vec = qv[:, :, 64 + 16 * ax:80 + 16 * ax].rearrange("p h (two n) -> p h two n", two=2)
                            cs = [rope[:, i, t, 8 * ax:8 * ax + 8].unsqueeze(1).to_broadcast([P, H, 8]) for i in range(2)]
                            ins = rotate(vec, 8, cs[0], cs[1])
                            if ax == 0:
                                link(ins)
                        ins.then_inc(s_qr, 1)
                    for hh in range(H):
                        dve.wait_ge(s_pr, prn + 1)
                        dve.wait_ge(s_pra, prn - 1)
                        src = pp[:, prn % 2, 0:keys]
                        link(v.tensor_reduce(mx[:, hh % 2, :], src, AX.X, ALU.max))
                        v.tensor_scalar(nb[:, hh % 2, :], mx[:, hh % 2, :], -SCALE, None, ALU.mult).then_inc(s_mx, 1)
                        prn += 1
                    dve.wait_ge(s_pv, u + 1)
                    dve.wait_ge(s_pra, prn)
                    link(v.reciprocal(ri[:, :], es[:, :]))
                    v.tensor_tensor(att[:, t, :].rearrange("p (h n) -> p h n", n=DK),
                                    pa[:, t % 2, :].rearrange("p (h n) -> p h n", n=DK),
                                    ri[:, :].unsqueeze(2).to_broadcast([P, H, DK]), ALU.mult).then_inc(s_att, 1)
                prn += 1
                dve.wait_ge(s_pra, prn)
                for j in range(N_OUT):
                    n = p * N_W + N_IN + j
                    dve.wait_ge(s_pj, n + 1)
                    cols = slice(j * P, (j + 1) * P)
                    tmp = xn[:, 0:P * nt].rearrange("p (t n) -> p t n", n=P)
                    link(v.tensor_tensor(tmp, pa[:, n % 2, 0:P * nt].rearrange("p (t n) -> p t n", n=P),
                                         gate[:, cols].unsqueeze(1).to_broadcast([P, nt, P]), ALU.mult))
                    v.tensor_tensor(xs[:, :, cols], xs[:, :, cols], tmp, ALU.add).then_inc(s_pjd, 1)
                    dve.wait_ge(s_pjd, p * N_OUT + j + 1)
                trn = tr_norm2(p)
                for t in range(nt):
                    if t:
                        dve.wait_ge(s_tp, trn + 4 * (t - 1) + 2)
                    norm(xs[:, t, :])
                prn += 1

                def top16(vals, idx, src, scratch):
                    link(v.max(vals[:, 0:8], src))
                    link(v.max_index(idx[:, 0:8], vals[:, 0:8], src))
                    link(v.match_replace(scratch, vals[:, 0:8], src, -3.0e38))
                    link(v.max(vals[:, 8:16], scratch))
                    link(v.max_index(idx[:, 8:16], vals[:, 8:16], scratch))

                def topk(u, hh):
                    for s in range(2):
                        top16(v16[:, s], i16[:, s], SS[:, 2 * hh + s, :], cand[:, 1, 0:NK])
                    link(v.tensor_copy(i16f[:, :, :], i16[:, :, :]))
                    cv = cand[:, 0, :].rearrange("p (a b) -> p a b", b=TOPK)
                    link(v.tensor_tensor(cv, v16[:, 0, :].unsqueeze(2).to_broadcast([P, TOPK, TOPK]),
                                         v16[:, 1, :].unsqueeze(1).to_broadcast([P, TOPK, TOPK]), ALU.add))
                    top16(bs[:, hh], pos, cand[:, 0, :], cand[:, 1, :])
                    link(v.tensor_scalar(ab[:, 0, :], pos[:, :], 4, None, ALU.logical_shift_right))
                    link(v.tensor_scalar(ab[:, 1, :], pos[:, :], TOPK - 1, None, ALU.bitwise_and))
                    link(v.tensor_copy(abf[:, :, :], ab[:, :, :]))
                    hot = cand[:, 0, :].rearrange("p (a b) -> p a b", b=TOPK)
                    for s in range(2):
                        link(v.tensor_tensor(hot, abf[:, s, :].unsqueeze(2).to_broadcast([P, TOPK, TOPK]),
                                             iota16[:, :].unsqueeze(1).to_broadcast([P, TOPK, TOPK]), ALU.is_equal))
                        link(v.tensor_tensor(hot, hot, i16f[:, s, :].unsqueeze(1).to_broadcast([P, TOPK, TOPK]), ALU.mult))
                        link(v.tensor_reduce(pick[:, s, :], hot, AX.X, ALU.add))
                    link(v.tensor_scalar(pick[:, 0, :], pick[:, 0, :], float(NK), float(l * EXPERTS), ALU.mult, ALU.add))
                    link(v.tensor_tensor(eidx[:, u % 2, hh * TOPK:(hh + 1) * TOPK], pick[:, 0, :], pick[:, 1, :], ALU.add))

                def shift_best():
                    link(v.tensor_copy(gs[:, 0, :], bs[:, :, 0]))
                    v.tensor_tensor(bs[:, :, :], bs[:, :, :], gs[:, 0, :].unsqueeze(2).to_broadcast([P, H, TOPK]),
                                    ALU.subtract).then_inc(s_bs, 1)

                def softmax(u):
                    dve.wait_ge(s_ge, u + 1)
                    link(v.tensor_reduce(gs[:, 0, :], gw[:, :, :], AX.X, ALU.add))
                    link(v.reciprocal(gs[:, 1, :], gs[:, 0, :]))
                    link(v.tensor_tensor(gw[:, :, :], gw[:, :, :], gs[:, 1, :].unsqueeze(2).to_broadcast([P, H, TOPK]),
                                         ALU.mult))

                for t in range(nt):
                    u = u0 + t
                    if t == 0:
                        dve.wait_ge(s_pra, prn + 2)
                        for hh in range(H):
                            topk(u, hh)
                        dve.sem_inc(s_tk, 1)
                        shift_best()
                    dve.wait_ge(s_te, tr_norm2(p) + 4 * nt)
                    softmax(u)
                    for k in range(H * TOPK):
                        dve.wait_ge(s_g[gn % GR], 16 * (gn // GR + 1))
                        v.tensor_tensor_reduce(ring[:, gn % GR, :], ring[:, gn % GR, :], h2[:, t, :], 1.0, 0.0,
                                               ALU.mult, ALU.add, dot[:, k:k + 1]).then_inc(s_gused, 1)
                        gn += 1
                    dve.wait_ge(s_gused, gn)
                    dve.sem_inc(s_dot, 1)
                    dve.wait_ge(s_gl, u + 1)
                    link(v.tensor_tensor(wv[:, :], gl[:, :], gw[:, :, :].rearrange("p h k -> p (h k)"), ALU.mult))
                    if t + 1 < nt:
                        dve.wait_ge(s_pra, prn + 2 * (t + 2))
                    for k in range(H * TOPK):
                        dve.wait_ge(s_g[gn % GR], 16 * (gn // GR + 1))
                        if k == 0:
                            ins = v.tensor_scalar(acc[:, :], ring[:, gn % GR, :], wv[:, 0:1], None, ALU.mult)
                        else:
                            dve.wait_ge(s_gused, gn)
                            ins = v.scalar_tensor_tensor(acc[:, :], ring[:, gn % GR, :], wv[:, k:k + 1], acc[:, :],
                                                         ALU.mult, ALU.add)
                        ins.then_inc(s_gused, 1)
                        gn += 1
                        if t + 1 < nt and k % TOPK == TOPK - 1:
                            topk(u + 1, k // TOPK)
                    if t + 1 < nt:
                        dve.sem_inc(s_tk, 1)
                        shift_best()
                    dve.wait_ge(s_gused, gn)
                    link(v.tensor_tensor(acc[:, :], acc[:, :], gate[:, :], ALU.mult))
                    link(v.tensor_tensor(xs[:, t, :], xs[:, t, :], acc[:, :], ALU.add))
                if l == DEPTH - 1:
                    for t in range(nt):
                        n = g * TILES[0] + t
                        if n:
                            dve.wait_ge(s_io, 16 * n)
                        norm(xs[:, t, :], frow[:, :])
                        dve.wait_ge(s_y, 2 * n + 1)
                        dve.sem_inc(s_y, 1)


def tr_count(p):
    nt, kt = NT[p], NT[p] + PASSES[p][0]
    return [2 * nt, 2 * nt, nt, kt, nt * (2 + H * (2 if kt > 4 else 1)), 2 * nt, 4 * nt]


def tr_before(p):
    return sum(sum(tr_count(q)) for q in range(p))


def tr_norm2(p):
    return tr_before(p) + sum(tr_count(p)[:-1])


def tr_hg(hu):
    p = max(q for q in range(4) if 2 * U0[q] <= hu)
    return tr_before(p) + 2 * NT[p] + hu - 2 * U0[p]


def pr_before(p):
    return sum(8 + NT[q] + PASSES[q][0] + NT[q] * (1 + H) + 2 + 2 * NT[q] for q in range(p))


def kernel(**inputs):
    import concourse.bacc as _bacc
    from concourse.bass_utils import run_bass_kernel_spmd as _run

    f = {k: np.ascontiguousarray(v) for k, v in inputs.items()}

    def tiles(w, n):
        return np.ascontiguousarray(w.reshape(DEPTH, KC, P, n, P).transpose(0, 3, 2, 1, 4))

    def rows(a):
        return np.ascontiguousarray(np.broadcast_to(a[None], (P,) + a.shape))

    inv = (1.0 / (10000.0 ** (np.arange(0, 16, 2, dtype=np.float32) / np.float32(16)))).astype(np.float32)
    tok = np.arange(DEC)
    ang = np.concatenate([(tok // 64).astype(np.float32)[:, None] * inv,
                          (tok % 64).astype(np.float32)[:, None] * inv], -1).astype(np.float32)
    table = np.stack([np.cos(ang), np.sin(ang)]).astype(np.float32)
    mk = masks()
    n_main = (N_IN - 1) * P
    arrays = {
        "ident": np.eye(P, dtype=np.float32),
        "masks": np.ascontiguousarray(mk.transpose(2, 0, 1, 3)),
        "maskf": np.ascontiguousarray(mk[:, 0].transpose(1, 0, 2)).astype(np.float32),
        "rope": np.ascontiguousarray(table.reshape(2, 4, P, 16).transpose(2, 0, 1, 3)),
        "cond": np.ascontiguousarray(np.stack([f["c_ctx"], f["c"][0]]).reshape(2, KC, P).transpose(2, 1, 0)),
        "b_ada": np.ascontiguousarray(f["b_ada"].reshape(DEPTH, N_ADA, P).transpose(2, 0, 1)),
        "nrm": np.ascontiguousarray(np.stack([f["norm_mix"], f["norm_ffn"]], 1).reshape(DEPTH, 2, KC, P)
                                    .transpose(3, 0, 1, 2)),
        "lbl": np.ascontiguousarray(f["hgrn_lb_logits"].reshape(2, DEPTH, 4, P).transpose(3, 0, 1, 2)),
        "x": np.ascontiguousarray(np.concatenate([f["x_prompt"][0], f["x_sample"][0]]).reshape(5, P, D)
                                  .transpose(1, 0, 2)),
        "qrow": rows(f["mla_q_norm"]), "kvrow": rows(f["mla_kv_norm"]), "hrow": rows(f["hgrn_norm"]),
        "frow": rows(f["final_norm"]),
        "w_ada": tiles(f["w_ada"], N_ADA),
        "w_in": tiles(np.ascontiguousarray(f["w_in"][:, :, :n_main]), N_IN - 1),
        "w_in_tail": np.ascontiguousarray(f["w_in"][:, :, n_main:].reshape(DEPTH, KC, P, ROPE).transpose(0, 2, 1, 3)),
        "w_out": tiles(f["w_out"], N_OUT),
        "w_q": tiles(f["peer_wq"], N_WQ),
        "wqb": np.ascontiguousarray(f["mla_wqb"].reshape(DEPTH, 3, P, H * DQ).transpose(0, 2, 1, 3)),
        "wkvb": np.ascontiguousarray(f["mla_wkvb"].reshape(DEPTH, 2, P, H * P).transpose(0, 2, 1, 3)),
        "keys": np.ascontiguousarray(f["peer_keys"].transpose(0, 4, 2, 1, 3).reshape(DEPTH, P, 2 * H, NK)),
        "cache_ckv": f["cache_ckv"][0], "cache_kpe": f["cache_kpe"][0],
        "state": np.ascontiguousarray(f["state_hgrn"][0].reshape(DEPTH, 2, 4, P, DK).transpose(0, 3, 1, 2, 4)),
        "peer_u": f["peer_u"].reshape(DEPTH * EXPERTS, D), "peer_v": f["peer_v"].reshape(DEPTH * EXPERTS, D),
    }
    outs = {"y": (5, P, D), "ckv": (DEPTH, P, KVL), "kpe": (DEPTH, P, ROPE), "state": (DEPTH, P, 2, 4, DK)}
    nc = _bacc.Bacc("TRN2", target_bir_lowering=False, num_devices=1)
    A = {k: nc.dram_tensor(f"in_{k}", v.shape, mybir.dt.from_np(v.dtype), kind="ExternalInput").ap()
         for k, v in arrays.items()}
    O = {k: nc.dram_tensor(f"out_{k}", s, F32, kind="ExternalOutput").ap() for k, s in outs.items()}
    build(nc, A, O)
    r = _run(nc, [{f"in_{k}": v for k, v in arrays.items()}], core_ids=[0]).results[0]
    y = r["out_y"].reshape(5 * P, D)
    state = r["out_state"].transpose(0, 2, 3, 1, 4).reshape(1, DEPTH, 2, H, DK, DK)
    return (y[None, :SEQ], y[None, SEQ:], r["out_ckv"][None], r["out_kpe"][None], state)
```

```python
from contextlib import ExitStack

import numpy as np

import concourse.bass as bass
from concourse import mybir

ALU = mybir.AluOpType
ACT = mybir.ActivationFunctionType
AX = mybir.AxisListType
F32 = mybir.dt.float32
I32 = mybir.dt.int32
U32 = mybir.dt.uint32
U8 = mybir.dt.uint8

P = 128
D = 1024
KC = D // P
DEPTH = 2
EPS = 1e-6
FLOOR = 1e-6
SEQ, DEC, PAST = 128, 512, 128
TILES = (SEQ // P, DEC // P)
PASSES = [(g, l) for l in range(DEPTH) for g in range(2)]
NT = [TILES[g] for g, _ in PASSES]
U0 = [sum(NT[:p]) for p in range(4)]
NU = sum(NT)
H, DK = 8, 64
QL, KVL, ROPE, DQ = 384, 256, 32, 96
SCALE = float(64 + 32) ** -0.5
NK, TOPK = 128, 16
EXPERTS = NK * NK
N_IN, N_OUT, N_WQ = 26, 8, 16
N_ADA, ADA = 48, 6
WR = 3
GR = 6
DR = 4
CH = 2
WCH = 2
NCH = H * TOPK // CH
LEVELS = (4, 8, 16, 32, 64)
LV = len(LEVELS) + 2
BATCHES = [[(0, 1)], [(0, 4)], [(0, 1)], [(0, 3), (3, 4)]]


def masks():
    s, t = np.arange(P)[:, None], np.arange(P)[None, :]
    out = np.zeros((2, 1 + len(LEVELS), P, P), np.int32)
    for d in range(2):
        a, b = (s, t) if d == 0 else (t, s)
        out[d, 0] = (s // 4 == t // 4) & (a <= b)
        for i, c in enumerate(LEVELS):
            out[d, 1 + i] = (s // (2 * c) == t // (2 * c)) & (a // c % 2 == 0) & (b // c % 2 == 1)
    return out


def trunk_steps():
    out = []

    def add(name, us, *args, need=None):
        out.append(((name, *args), us, need))

    for i in range(N_ADA // ADA):
        add("ada", 10, 0, i)
    add("adafin", 1, 0)
    for p, (g, l) in enumerate(PASSES):
        nt, u0, big = NT[p], U0[p], 3.5 if g else 1
        for b, (t0, t1) in enumerate(BATCHES[p]):
            for t in range(t0, t1):
                add("norm", 8, p, t, 0, need=("fin", u0 - 5 + g * 0 + t) if l else None)
            for j in range(N_IN):
                add("inp", 2 * max(1, (t1 - t0) * 0.9), p, b, j)
                if p == 1 and j % 3 == 2:
                    add("ada", 10, 1, j // 3)
            if p == 1:
                add("adafin", 1, 1)
            if b == 0:
                add("small", 0, p)
            add("fgate", 4, p, b)
            for t in range(t0, t1):
                for m in range(LV):
                    add("hg", 7.5, p, 0, t, m)
        for t in reversed(range(nt)):
            for m in range(LV):
                add("hg", 7.5, p, 1, t, m)
        for t in range(nt):
            add("hgfin", 4, p, t)
        add("latn", 3 + 3 * nt, p)
        add("latT", 3 * nt, p)
        add("kn", 10 * big, p)
        add("va", 4 * big, p)
        for t in range(nt):
            u = u0 + t
            add("q", 10, p, t)
            add("sc", 2, p, t, 0)
            for hh in range(H):
                if hh + 1 < H:
                    add("sc", 2, p, t, hh + 1)
                add("pv", 3, p, t, hh)
            for i in range(N_OUT // WCH):
                add("outp", 6, p, t, i)
            add("norm", 10, p, t, 1, need=("gelu", u - 2) if u >= 2 else None)
            for i in range(N_WQ // WCH):
                add("wq", 4.5, p, t, i)
            add("score", 8, p, t)
            for hh in range(H):
                add("topk", 7.5, u, hh, need=("fin", u - 3) if u >= 3 else None)
            add("soft", 2, u)
    return out


def peer_steps(done):
    part = [0] * (NU + 1)
    for u in range(NU):
        while part[u] < NCH:
            yield ("u", u, part[u]), 1.5 * CH, ("soft", u)
            part[u] += 1
        yield ("gelu", u), 3, None
        if u == NU - 1:
            for w in range(NU - 5, NU - 1):
                yield ("y", w), 3, None
        for c in range(NCH):
            yield ("v", u, c), 1.7 * CH, None
            if u + 1 < NU and ("soft", u + 1) in done and part[u + 1] < NCH:
                yield ("u", u + 1, part[u + 1]), 1.5 * CH, None
                part[u + 1] += 1
        yield ("fin", u), 3, None
    yield ("y", NU - 1), 3, None


def plan():
    out, done = [], set()
    trunk, peer = trunk_steps(), peer_steps(done)
    clock, i = [0.0, 0.0], 0
    nxt = next(peer)
    while i < len(trunk) or nxt is not None:
        ok = [i < len(trunk) and (trunk[i][2] is None or trunk[i][2] in done),
              nxt is not None and (nxt[2] is None or nxt[2] in done)]
        name, *a = trunk[i][0] if i < len(trunk) else ("end",)
        if nxt is not None and nxt[0][0] == "fin" and name in ("outp", "wq") and a[2] * WCH % 8:
            ok[1] = False
        assert any(ok)
        w = min((x for x in (0, 1) if ok[x]), key=lambda x: clock[x])
        if not ok[1 - w]:
            clock[1 - w] = max(clock[1 - w], clock[w])
        step, us = (trunk[i] if w == 0 else nxt)[:2]
        clock[w] += us
        out.append(step)
        done.add(step)
        done.add(step[:2])if step[0] in ("fin", "gelu", "soft") else None
        if w == 0:
            i += 1
        else:
            nxt = next(peer, None)
    return out


PLAN = plan()


def raises(step):
    name, a = step[0], step[1:]
    if name == "ada":
        return {"it": 1, "id": 1, "wu": ADA - 1}
    if name == "adafin":
        return {"mods": 1}
    if name == "norm":
        n = 4 if a[2] else 2
        return {"ms": 1, "rt": 1, "xn": 1, "tp": n, "te": n}
    if name == "inp":
        return {"it": 1, "ia": 1}
    if name == "hg":
        out = {"it": 1, "id": 1, "lv": (2, *[1] * (LV - 2), 0)[a[3]]}
        return out | ({"tp": 1, "te": 1, "o": 1, "S": 1, "hgn": 1} if a[3] == LV - 1 else {})
    if name == "hgfin":
        return {"ms": 1, "rt": 1, "hg": 1}
    if name == "latn":
        return {"ms": 1, "rt": 1, "cn": 1}
    if name == "latT":
        p = a[0]
        n = 2 * NT[p] + PASSES[p][0]
        return {"tp": n, "te": n}
    if name in ("kn", "va"):
        n = H if name == "kn" else NT[a[0]] + PASSES[a[0]][0]
        return {"it": n, "ia": n}
    if name == "q":
        return {"it": 1, "ia": 1, "tp": 2, "te": 2, "qr": PASSES[a[0]][0]}
    if name == "sc":
        return {"it": 1, "ia": 1, "mx": 1}
    if name == "pv":
        n = 2 if NT[a[0]] + PASSES[a[0]][0] > 4 else 1
        return {"tp": n, "te": n, "pv": 1, "td": 1}
    if name == "outp":
        if a[2] == 0:
            return {"it": 1, "ia": 1, "tp": 2, "te": 2, "wu": WCH}
        return {"it": 1, "id": 1, "wu": WCH - 1} if a[2] == N_OUT // WCH - 1 else {"wu": WCH}
    if name == "wq":
        half = N_WQ // WCH // 2
        return {"it": 1, "ia": 1, "wu": WCH - 1} if a[2] % half == half - 1 else {"wu": WCH}
    if name == "score":
        return {"it": 2, "ia": 2}
    if name == "soft":
        return {"tk": 1, "ge": 1}
    if name == "u":
        return {"gu": CH}
    if name == "gelu":
        return {"dot": 1, "gl": 1, "wv": 1}
    if name == "v":
        return {"dg": CH, "gv": CH}
    if name == "fin":
        return {"it": 1, "ia": 1, "xr": 1}
    if name == "y":
        return {"ms": 1, "rt": 1, "y": 1}
    return {}


def tally():
    out, now = [], {}
    for step in PLAN + [("end",)]:
        out.append(dict(now))
        for name, n in raises(step).items():
            now[name] = now.get(name, 0) + n
    return out


TALLY = tally()
PLACE = {step: k for k, step in enumerate(PLAN)}


def before(k, name):
    return TALLY[k].get(name, 0)


def after(step, name):
    return TALLY[PLACE[step] + 1].get(name, 0)


def weight_tiles():
    out = []
    for k, step in enumerate(PLAN):
        name, a = step[0], step[1:]
        it, wu = before(k, "it"), before(k, "wu")
        if name == "ada":
            srcs = [("w_ada", (a[0], a[1] * ADA + i)) for i in range(ADA)]
        elif name == "inp":
            p, _, j = a
            l = PASSES[p][1]
            srcs = [("w_in", (l, j))] if j < N_IN - 1 else [("w_in_tail", (l,))]
        elif name == "outp":
            srcs = [("w_out", (PASSES[a[0]][1], a[2] * WCH + j)) for j in range(WCH)]
        elif name == "wq":
            srcs = [("w_q", (PASSES[a[0]][1], a[2] * WCH + j)) for j in range(WCH)]
        else:
            continue
        for i, (array, index) in enumerate(srcs):
            used = ("wu", wu + i + 1) if i < raises(step).get("wu", 0) else ("it", it + 1)
            out.append((array, index, used, k))
    return out


def gathers():
    out = []
    for k, step in enumerate(PLAN):
        if step[0] in ("u", "v"):
            name = "gu" if step[0] == "u" else "gv"
            for i in range(CH):
                out.append((step[1], step[2] * CH + i, "peer_" + step[0], (name, before(k, name) + i + 1)))
    return out


WEIGHTS = weight_tiles()
GATHERS = gathers()
GATHER_AT = {}
for _n, _x in enumerate(GATHERS):
    GATHER_AT[_x[2], _x[0], _x[1]] = _n


def build(nc, A, O):
    with ExitStack() as ctx:
        def sb(name, shape, dt=F32):
            return ctx.enter_context(nc.sbuf_tensor(name, shape, dt))

        def ps(name, shape):
            return ctx.enter_context(nc.psum_tensor(name, shape, F32))

        def sem(name):
            return ctx.enter_context(nc.semaphore(name))

        x = sb("x", [P, 5, D])
        gate = sb("gate", [P, D])
        hT = sb("hT", [P, KC, DEC])
        hflat = hT[:, :, :].rearrange("p a b -> p (a b)")
        cqT = hT[:, 0:3, :]
        ckvT = hflat[:, 1536:2816].rearrange("p (a b) -> p a b", a=2)
        mT = hflat[:, 3072:4096].rearrange("p (c t) -> p c t", t=P)
        wring = sb("wring", [P, WR, KC, P])
        wqb = sb("wqb", [P, 3, H * DQ])
        wkvb = sb("wkvb", [P, 2, H * P])
        keysT = wkvb[:, :, :].rearrange("p c (s k) -> p (c s) k", k=NK)
        U = sb("U", [P, 11264])
        sigq = U[:, 0:6144].rearrange("p (a t) -> p a t", t=DEC)
        Kt = U[:, 6144:6656].rearrange("p (g t) -> p g t", t=P)
        Pt = U[:, 6656:7168].rearrange("p (g t) -> p g t", t=P)
        Xt = U[:, 7168:7680].rearrange("p (g t) -> p g t", t=P)
        QP = U[:, 7680:8704].rearrange("p (b g t) -> p b g t", b=2, t=P)
        KX = U[:, 8704:9728].rearrange("p (b g t) -> p b g t", b=2, t=P)
        Asb = U[:, 9728:10752].rearrange("p (e g t) -> p e g t", e=2, t=P)
        KTn = U[:, 10752:11264].rearrange("p (g t) -> p g t", t=P)
        kT = U[:, 0:5120].rearrange("p (h k) -> p h k", h=H)
        vatt = U[:, 5120:7680].rearrange("p (a n) -> p a n", n=512)
        Pn = U[:, 7680:8960].rearrange("p (b k) -> p b k", b=2)
        qn = U[:, 7680:8448]
        PT = U[:, 8960:10240].rearrange("p (b a t) -> p b a t", b=2, t=P)
        QT = U[:, 10240:11264].rearrange("p (h t) -> p h t", t=P)
        V = sb("V", [P, 4, 512])
        att = V
        GT = sb("GT", [P, 4, 512])
        qpT = GT[:, :, :].rearrange("p a b -> p (a b)").rearrange("p (a t) -> p a t", t=P)
        o = sb("o", [P, 4, 512])
        lat = sb("lat", [P, 2976])
        cq = lat[:, 0:1536].rearrange("p (t n) -> p t n", n=QL)
        ckv = lat[:, 1536:2816].rearrange("p (t n) -> p t n", n=KVL)
        kpe = lat[:, 2816:2976].rearrange("p (t n) -> p t n", n=ROPE)
        SS = lat[:, 0:2048].rearrange("p (a k) -> p a k", k=NK)
        xn = sb("xn", [P, D])
        rt = xn[:, 0:512].rearrange("p (i n) -> p i n", i=4)
        ring = sb("ring", [P, GR, D])
        h2 = sb("h2", [P, 2, D])
        dgw = sb("dgw", [P, DR, P])
        S = sb("S", [P, 2, 4, DK])
        ident = sb("ident", [P, P])
        mk = sb("mk", [P, 2, 6, P], U8)
        maskf = sb("maskf", [P, 2, P])
        rope = sb("rope", [P, 2, 4, 16])
        cond = sb("cond", [P, KC, 2])
        bada = sb("bada", [P, DEPTH, N_ADA])
        nrm = sb("nrm", [P, DEPTH, 2, KC])
        mods = sb("mods", [P, DEPTH, N_ADA, 2])
        Am = sb("Am", [P, DEPTH, 2, KC, 2])
        lbl = sb("lbl", [P, 2, DEPTH, 4])
        lb = sb("lb", [P, 2, DEPTH, 4])
        omlb = sb("omlb", [P, 2, DEPTH, 4])
        lt = sb("lt", [P, 4, 2, 4])
        qrow = sb("qrow", [P, QL])
        kvrow = sb("kvrow", [P, KVL])
        hrow = sb("hrow", [P, DEPTH, DK])
        frow = U[:, 0:D]
        yt = U[:, D:3 * D].rearrange("p (b d) -> p b d", b=2)
        st = sb("st", [P, 4])
        sty = sb("sty", [P, 4])
        st8 = sb("st8", [P, 4, 8])
        mx = sb("mx", [P, 2, 1])
        nb = sb("nb", [P, 2, 1])
        es = sb("es", [P, H])
        ri = sb("ri", [P, H])
        v16 = sb("v16", [P, 2, TOPK])
        i16 = sb("i16", [P, 2, TOPK], U32)
        i16f = sb("i16f", [P, 2, TOPK])
        cand = sb("cand", [P, 2, TOPK * TOPK])
        pos = sb("pos", [P, TOPK], U32)
        ab = sb("ab", [P, 2, TOPK], U32)
        abf = sb("abf", [P, 2, TOPK])
        iota16 = sb("iota16", [P, TOPK])
        pick = sb("pick", [P, 2, TOPK])
        bs = sb("bs", [P, H, TOPK])
        gw = sb("gw", [P, 3, H, TOPK])
        gs = sb("gs", [P, 2, H])
        eidx = sb("eidx", [P, 3, H * TOPK], I32)
        dot = sb("dot", [P, H * TOPK])
        gl = sb("gl", [P, H * TOPK])
        wv = sb("wv", [P, H * TOPK])

        acc = ps("acc", [P, D])
        tb = ps("tb", [P, 2, 512])
        pp = ps("pp", [P, 2, 1024])

        s_const = sem("s_const")
        s_cond = sem("s_cond")
        s_lbd = sem("s_lbd")
        s_lbe = sem("s_lbe")
        s_w = [sem(f"s_w{i}") for i in range(WR)]
        s_sw = sem("s_sw")
        s_keys = sem("s_keys")
        s_Sst = sem("s_Sst")
        s_out = sem("s_out")
        s_frow = sem("s_frow")
        s_yst = [sem(f"s_yst{i}") for i in range(2)]
        s_g = [sem(f"s_g{i}") for i in range(GR)]
        c_dve = sem("c_dve")
        C = {name: sem("s_" + name) for name in (
            "it",
            "ia",
            "id",
            "tp",
            "te",
            "td",
            "wu",
            "mods",
            "ms",
            "rt",
            "xn",
            "lv",
            "o",
            "S",
            "hgn",
            "hg",
            "cn",
            "qr",

            "mx",
            "pv",
            "tk",
            "ge",
            "gu",
            "dot",
            "gl",
            "wv",
            "dg",
            "gv",
            "xr",
            "y",
        )}

        consts = [(ident[:, :], A["ident"]), (cond[:, :, :], A["cond"]), (bada[:, :, :], A["b_ada"]),
                  (nrm[:, :, :, :], A["nrm"]), (lbl[:, :, :, :], A["lbl"]), (x[:, :, :], A["x"]),
                  (U[:, 0:2 * 6 * P].bitcast(I32).rearrange("p (d m t) -> p d m t", d=2, t=P), A["masks"]),
                  (maskf[:, :, :], A["maskf"]),
                  (rope[:, :, :, :], A["rope"]), (hrow[:, :, :], A["hrow"])]
        CONST = 16 * len(consts)

        def n_small(p):
            return sum(4 + 3 * PASSES[i][0] for i in range(p + 1))

        block = ctx.enter_context(nc.Block())

        @block.sync
        def _(sp):
            for dst, src in consts:
                sp.dma_start(dst, src).then_inc(s_const, 16)
            n = 0
            for k, step in enumerate(PLAN):
                name, a = step[0], step[1:]
                while n < len(WEIGHTS) and WEIGHTS[n][3] == k:
                    array, index, _, _ = WEIGHTS[n]
                    if n >= WR:
                        which, value = WEIGHTS[n - WR][2]
                        sp.wait_ge(C[which], value)
                    src = A[array]
                    for i in index:
                        src = src[i]
                    dst = wring[:, n % WR, :, 0:src.shape[2]] if src.shape[2] < P else wring[:, n % WR]
                    sp.dma_start(dst, src).then_inc(s_w[n % WR], 16)
                    n += 1
                if name == "small":
                    p, = a
                    g, l = PASSES[p]
                    if p:
                        sp.wait_ge(C["it"], after(("score", p - 1, NT[p - 1] - 1), "it"))
                        sp.wait_ge(C["tk"], U0[p])
                    sp.dma_start(wqb[:, :, :], A["wqb"][l]).then_inc(s_sw, 16)
                    sp.dma_start(wkvb[:, :, :], A["wkvb"][l]).then_inc(s_sw, 16)
                    sp.dma_start(qrow[:, :], A["qrow"][l]).then_inc(s_sw, 16)
                    sp.dma_start(kvrow[:, :], A["kvrow"][l]).then_inc(s_sw, 16)
                    if g:
                        sp.dma_start(ckv[:, 0, :], A["cache_ckv"][l]).then_inc(s_sw, 16)
                        sp.dma_start(kpe[:, 0, :], A["cache_kpe"][l]).then_inc(s_sw, 16)
                        sp.wait_ge(s_Sst, 16 * (l + 1))
                        sp.dma_start(S[:, :, :, :], A["state"][l]).then_inc(s_sw, 16)
                elif name == "latn" and not PASSES[a[0]][0]:
                    l = PASSES[a[0]][1]
                    sp.wait_ge(C["S"], before(k, "S"))
                    sp.dma_start(O["state"][l], S[:, :, :, :]).then_inc(s_Sst, 16)
                    sp.wait_ge(C["cn"], before(k, "cn") + 1)
                    sp.dma_start(O["ckv"][l], ckv[:, 0, :]).then_inc(s_out, 16)
                    sp.dma_start(O["kpe"][l], kpe[:, 0, :]).then_inc(s_out, 16)
                elif name == "va":
                    p = a[0]
                    sp.wait_ge(C["it"], before(k + 1, "it"))
                    sp.dma_start(keysT, A["keys"][PASSES[p][1]]).then_inc(s_keys, 16)
                elif name == "y":
                    i = a[0] - (NU - 5)
                    if i == 0:
                        sp.wait_ge(C["it"], after(("sc", 3, NT[3] - 1, H - 1), "it"))
                        sp.wait_ge(C["td"], before(len(PLAN), "td"))
                        sp.dma_start(frow, A["frow"]).then_inc(s_frow, 16)
                    sp.wait_ge(C["y"], i + 1)
                    sp.dma_start(O["y"][i], yt[:, i % 2, :]).then_inc(s_yst[i % 2], 16)
            sp.wait_ge(s_out, 16 * 4)
            sp.wait_ge(s_Sst, 16 * 2)
            sp.wait_ge(s_yst[0], 16 * 3)
            sp.wait_ge(s_yst[1], 16 * 2)

        @block.gpsimd
        def _(pool):
            pool.iota(iota16[:, :], [[1, TOPK]], base=0, channel_multiplier=0,
                      allow_small_or_imprecise_dtypes=True).then_inc(s_const, 16)
            for n, (u, col, table, _) in enumerate(GATHERS):
                if col == 0 and table == "peer_u":
                    pool.wait_ge(C["tk"], u + 1)
                if n >= GR:
                    which, value = GATHERS[n - GR][3]
                    pool.wait_ge(C[which], value)
                pool.indirect_dma_start(ring[:, n % GR, :], None, A[table],
                                        bass.IndirectOffsetOnAxis(ap=eidx[:, u % 3, col:col + 1], axis=0),
                                        ).then_inc(s_g[n % GR], 16)

        def landed(eng, table, u, col):
            n = GATHER_AT[table, u, col]
            eng.wait_ge(s_g[n % GR], 16 * (n // GR + 1))
            return ring[:, n % GR, :]

        @block.tensor
        def _(pe):
            wn = 0
            open_pair = None
            items, banks = [], []
            freed = {"ia": 0, "id": 0, "te": 0, "td": 0}

            def wtile():
                nonlocal wn
                pe.wait_ge(s_w[wn % WR], 16 * (wn // WR + 1))
                wn += 1
                return wring[:, (wn - 1) % WR]

            def pair(by):
                n = len(items)
                if n >= 2:
                    pe.wait_ge(C[items[n - 2][0]], items[n - 2][1])
                freed[by] += 1
                items.append((by, freed[by]))
                return pp[:, n % 2, :]

            def transposes(pieces, signal=True):
                n = len(banks)
                if n >= 2:
                    pe.wait_ge(C[banks[n - 2][0]], banks[n - 2][1])
                freed["te"] += 1
                banks.append(("te", freed["te"]))
                for i, piece in enumerate(pieces):
                    m = piece.shape[1]
                    ins = nc.tensor.transpose(tb[0:m, n % 2, i * P:(i + 1) * P], piece, ident[:, :])
                ins.then_inc(C["tp"], 1)
                return n % 2

            def copied():
                pe.wait_ge(C["te"], freed["te"])

            def gate_row(which, g, l):
                b = pair("ia")
                for c in range(KC):
                    col = mods[:, l, (2 + 3 * which) * KC + c, g:g + 1]
                    ins = nc.tensor.matmul(b[:, c * P:(c + 1) * P], col.to_broadcast([P, P]), ident[:, :],
                                           start=True, stop=True)
                ins.then_inc(C["it"], 1)

            def norm(k, p, t, which):
                pe.wait_ge(C["xn"], before(k, "xn") + 1)
                for i in range(2):
                    transposes([xn[:, (4 * i + c) * P:(4 * i + c + 1) * P] for c in range(4)])
                if which:
                    copied()
                    for i in range(2):
                        transposes([mT[:, 4 * i + c, :] for c in range(4)])

            def project(k, p, b, j):
                t0, t1 = BATCHES[p][b]
                if j == 0:
                    copied()
                wt = wtile()
                out = pair("ia")
                if j < 12:
                    n = (t1 - t0) * P
                    for c in range(KC):
                        ins = nc.tensor.matmul(out[:, 0:n], wt[:, c, :], hT[:, c, t0 * P:t1 * P],
                                               start=(c == 0), stop=(c == KC - 1))
                else:
                    m = P if j < N_IN - 1 else ROPE
                    for t in range(t0, t1):
                        for c in range(KC):
                            ins = nc.tensor.matmul(out[:, (t - t0) * P:(t - t0) * P + m], hT[:, c, t * P:(t + 1) * P],
                                                   wt[:, c, 0:m], start=(c == 0), stop=(c == KC - 1))
                ins.then_inc(C["it"], 1)

            def recurrence(k, p, d, t, m):
                lv = before(PLACE["hg", p, d, t, 0], "lv")
                if m == 0:
                    pe.wait_ge(C["ia"], freed["ia"])
                out = pair("id")
                pe.wait_ge(C["lv"], lv + m + 1)
                if m < LV - 1:
                    for gg in range(4):
                        for e in range(2):
                            r = slice(64 * e, 64 * e + 64)
                            ins = nc.tensor.matmul(out[:, e * 512 + gg * P:e * 512 + (gg + 1) * P],
                                                   KX[r, (lv + m) % 2, gg, :], QP[r, (lv + m) % 2, gg, :],
                                                   start=True, stop=True)
                    ins.then_inc(C["it"], 1)
                    return
                last = (lv + m) % 2
                transposes([KX[:, last, gg, :] for gg in range(4)])
                pe.wait_ge(C["hgn"], before(k, "hgn") + 1)
                if before(k, "S"):
                    pe.wait_ge(C["S"], before(k, "S"))
                if PASSES[p][0]:
                    pe.wait_ge(s_sw, 16 * n_small(p))
                for gg in range(4):
                    for e in range(2):
                        hh = 2 * gg + e
                        r = slice(64 * e, 64 * e + 64)
                        dst = out[:, e * 512 + gg * DK:e * 512 + (gg + 1) * DK]
                        nc.tensor.matmul(dst, Asb[:, e, gg, :], V[:, t, hh * DK:(hh + 1) * DK], start=True, stop=False)
                        ins = nc.tensor.matmul(dst, QP[r, last, gg, :], S[r, d, gg, :], start=False, stop=True)
                ins.then_inc(C["o"], 1)
                copied()
                for gg in range(4):
                    for e in range(2):
                        hh = 2 * gg + e
                        ins = nc.tensor.matmul(out[64 * e:64 * e + 64, 256 + gg * DK:256 + (gg + 1) * DK],
                                               KTn[:, gg, 64 * e:64 * e + 64], V[:, t, hh * DK:(hh + 1) * DK],
                                               start=True, stop=True)
                ins.then_inc(C["it"], 1)

            def latents_T(k, p):
                g = PASSES[p][0]
                pe.wait_ge(C["cn"], before(k, "cn"))
                pe.wait_ge(s_sw, 16 * n_small(p))
                for t in range(NT[p]):
                    transposes([cq[:, t, i * P:(i + 1) * P] for i in range(3)])
                for t in range(NT[p] + g):
                    transposes([ckv[:, t, i * P:(i + 1) * P] for i in range(2)] + [kpe[:, t, :]])
                copied()

            def keys_T(k, p):
                keys = (NT[p] + PASSES[p][0]) * P
                for hh in range(H):
                    b = pair("ia")
                    for k0 in range(0, keys, 512):
                        kn = min(512, keys - k0)
                        for c in range(2):
                            ins = nc.tensor.matmul(b[0:64, k0:k0 + kn], wkvb[:, c, hh * P:hh * P + 64],
                                                   ckvT[:, c, k0:k0 + kn], start=(c == 0), stop=(c == 1))
                    ins.then_inc(C["it"], 1)

            def values(k, p):
                w4 = wkvb[:, :, :].rearrange("p c (h n) -> p c h n", h=H)
                for t in range(NT[p] + PASSES[p][0]):
                    b = pair("ia")
                    for c in range(2):
                        ins = nc.tensor.matmul(b[:, 0:512].rearrange("p (h n) -> p h n", h=H),
                                               ckvT[:, c, t * P:(t + 1) * P], w4[:, c, :, 64:128],
                                               start=(c == 0), stop=(c == 1))
                    ins.then_inc(C["it"], 1)

            def queries(k, p, t):
                b = pair("ia")
                for half in range(2):
                    for c in range(3):
                        ins = nc.tensor.matmul(b[:, half * 512:half * 512 + QL], cqT[:, c, t * P:(t + 1) * P],
                                               wqb[:, c, half * QL:(half + 1) * QL], start=(c == 0), stop=(c == 2))
                ins.then_inc(C["it"], 1)
                pe.wait_ge(C["ia"], freed["ia"])
                if PASSES[p][0]:
                    pe.wait_ge(C["qr"], before(k, "qr") + 1)
                for i in range(2):
                    transposes([qn[:, (4 * i + c) * DQ:(4 * i + c + 1) * DQ] for c in range(4)])
                copied()

            def scores(k, p, t, hh):
                keys = (NT[p] + PASSES[p][0]) * P
                b = pair("ia")
                for k0 in range(0, keys, 512):
                    kn = min(512, keys - k0)
                    ins = nc.tensor.matmul(b[:, k0:k0 + kn], QT[0:DQ, hh, :], kT[0:DQ, hh, k0:k0 + kn],
                                           start=True, stop=True)
                ins.then_inc(C["it"], 1)

            def head(k, p, t, hh):
                kt_n = NT[p] + PASSES[p][0]
                hi = hh % 2
                pe.wait_ge(C["ia"], after(("sc", p, t, hh), "ia"))
                bank = transposes([Pn[:, hi, a * P:(a + 1) * P] for a in range(min(4, kt_n))])
                if kt_n > 4:
                    bank = transposes([Pn[:, hi, 4 * P:5 * P]])
                freed["td"] += 1
                banks[-1] = ("td", freed["td"])
                copied()
                for a in range(kt_n):
                    ins = nc.tensor.matmul(tb[:, bank, 256:256 + DK], PT[:, hi, a, :], vatt[:, a, hh * DK:(hh + 1) * DK],
                                           start=(a == 0), stop=(a == kt_n - 1))
                ins.then_inc(C["pv"], 1)

            def project_chunk(i, by, product):
                nonlocal open_pair
                if i * WCH % 8 == 0:
                    open_pair = pair(by)
                for j in range(i * WCH, (i + 1) * WCH):
                    wt = wtile()
                    for c in range(KC):
                        ins = product(open_pair[:, j % 8 * P:(j % 8 + 1) * P], wt[:, c, :], mT[:, c, :], c)
                    ins.then_inc(C["it"] if j % 8 == 7 else C["wu"], 1)

            def output(k, p, t, i):
                if i == 0:
                    g, l = PASSES[p]
                    gate_row(0, g, l)
                    pe.wait_ge(C["hg"], before(k, "hg"))
                    transposes([o[:, t, c * P:(c + 1) * P] for c in range(4)])
                    pe.wait_ge(C["td"], freed["td"])
                    transposes([att[:, t, c * P:(c + 1) * P] for c in range(4)])
                    copied()
                project_chunk(i, "id", lambda out, w, m, c: nc.tensor.matmul(
                    out, m, w, start=(c == 0), stop=(c == KC - 1)))

            def peer_queries(k, p, t, i):
                if i == 0:
                    copied()
                project_chunk(i, "ia", lambda out, w, m, c: nc.tensor.matmul(
                    out, w, m, start=(c == 0), stop=(c == KC - 1)))

            def sub_key_scores(k, p, t):
                pe.wait_ge(C["ia"], freed["ia"])
                pe.wait_ge(s_keys, 16 * (p + 1))
                for i in range(2):
                    b = pair("ia")
                    for a in range(8):
                        ins = nc.tensor.matmul(b[:, a * P:(a + 1) * P], qpT[:, 8 * i + a, :], keysT[:, 8 * i + a, :],
                                               start=True, stop=True)
                    ins.then_inc(C["it"], 1)

            def modulation(k, l, i):
                out = pair("id")
                for j in range(ADA):
                    wt = wtile()
                    for c in range(KC):
                        ins = nc.tensor.matmul(out[:, 2 * j:2 * j + 2], wt[:, c, :], cond[:, c, :],
                                               start=(c == 0), stop=(c == KC - 1))
                    ins.then_inc(C["wu"] if j < ADA - 1 else C["it"], 1)

            def sum_v(k, u, c):
                if c == 0 and u:
                    pe.wait_ge(C["xr"], u)
                for i in range(CH):
                    n = before(k, "gv") + i
                    rows = landed(pe, "peer_v", u, c * CH + i)
                    pe.wait_ge(C["dg"], n + 1)
                    for half in range(2):
                        ins = nc.tensor.matmul(acc[:, half * 512:(half + 1) * 512], dgw[:, n % DR, :],
                                               rows[:, half * 512:(half + 1) * 512],
                                               start=(c + i == 0), stop=(c == NCH - 1 and i == CH - 1))
                    ins.then_inc(C["gv"], 1)

            def finish(k, u):
                p = max(q for q in range(4) if U0[q] <= u)
                gate_row(1, *PASSES[p])

            pe.wait_ge(s_const, CONST + 16)
            pe.wait_ge(s_cond, 1)
            do = {"norm": norm, "inp": project, "hg": recurrence, "latT": latents_T, "kn": keys_T, "va": values,
                  "q": queries, "sc": scores, "pv": head, "outp": output, "wq": peer_queries, "score": sub_key_scores,
                  "ada": modulation, "v": sum_v, "fin": finish}
            for k, step in enumerate(PLAN):
                if step[0] in do:
                    do[step[0]](k, *step[1:])

        @block.scalar
        def _(act):
            def got_t(n):
                act.wait_ge(C["tp"], n + 1)
                return tb[:, n % 2, :].rearrange("p (c t) -> p c t", t=P)

            def got_pair(n):
                act.wait_ge(C["it"], n + 1)
                return pp[:, n % 2, :]

            def copy(dst, src, **kw):
                return nc.scalar.activation(dst, src, ACT.Copy, **kw)

            def root(k, dst, src):
                act.wait_ge(C["ms"], before(k, "ms") + 1)
                nc.scalar.activation(dst, src, ACT.Sqrt).then_inc(C["rt"], 1)

            def norm(k, p, t, which):
                g, l = PASSES[p]
                if which == 0 and t == 0:
                    act.wait_ge(C["mods"], l + 1)
                root(k, st[:, 2:3], st[:, 1:2])
                n = before(k, "tp")
                for i in range(2):
                    src = got_t(n + i)
                    for c in range(4):
                        kc = 4 * i + c
                        dst = mT[:, kc, :] if which else hT[:, kc, t * P:(t + 1) * P]
                        ins = nc.scalar.activation(dst, src[:, c, :], ACT.Identity, scale=Am[:, l, which, kc, g:g + 1],
                                                   bias=mods[:, l, 3 * which * KC + kc, g:g + 1])
                    ins.then_inc(C["te"], 1)
                if which:
                    u = U0[p] + t
                    if u >= 2:
                        act.wait_ge(C["gu"], H * TOPK * (u - 1))
                    for i in range(2):
                        src = got_t(n + 2 + i)
                        copy(h2[:, u % 2, 512 * i:512 * (i + 1)].rearrange("p (c t) -> p c t", t=P), src)\
                            .then_inc(C["te"], 1)

            def project(k, p, b, j):
                g = PASSES[p][0]
                t0, t1 = BATCHES[p][b]
                nt, w = t1 - t0, (t1 - t0) * P
                src = got_pair(before(k, "it"))
                nat = src.rearrange("p (t n) -> p t n", n=P)[:, 0:nt, :]
                cols = slice(t0 * P, t1 * P)
                if j < 4:
                    ins = copy(sigq[:, j, cols], src[:, 0:w], scale=DK ** -0.5)
                elif j < 12:
                    ins = nc.scalar.activation(sigq[:, j, cols], src[:, 0:w], ACT.Sigmoid)
                elif j < 16:
                    ins = copy(V[:, t0:t1, (j - 12) * P:(j - 11) * P], nat)
                elif j < 20:
                    ins = nc.scalar.activation(GT[:, t0:t1, (j - 16) * P:(j - 15) * P], nat, ACT.Silu)
                elif j < 23:
                    ins = copy(cq[:, t0:t1, (j - 20) * P:(j - 19) * P], nat)
                elif j < 25:
                    ins = copy(ckv[:, g + t0:g + t1, (j - 23) * P:(j - 22) * P], nat)
                else:
                    ins = copy(kpe[:, g + t0:g + t1, :], nat[:, :, 0:ROPE])
                ins.then_inc(C["ia"], 1)

            def recurrence(k, p, d, t, m):
                if m == LV - 1:
                    src = got_t(before(k, "tp"))
                    copy(KTn[:, :, :], src).then_inc(C["te"], 1)

            def latents(k, p):
                root(k, st8[:, 2, :], st8[:, 1, :])

            def out_norm(k, p, t):
                root(k, st8[:, 2, :], st8[:, 1, :])

            def latents_T(k, p):
                n = before(k, "tp")
                for t in range(NT[p]):
                    copy(cqT[:, :, t * P:(t + 1) * P], got_t(n)[:, 0:3, :]).then_inc(C["te"], 1)
                    n += 1
                for t in range(NT[p] + PASSES[p][0]):
                    src = got_t(n)
                    n += 1
                    copy(ckvT[:, :, t * P:(t + 1) * P], src[:, 0:2, :])
                    copy(kT[64:96, :, t * P:(t + 1) * P],
                         src[0:ROPE, 2:3, :].to_broadcast([ROPE, H, P])).then_inc(C["te"], 1)

            def keys_T(k, p):
                keys = (NT[p] + PASSES[p][0]) * P
                for hh in range(H):
                    copy(kT[0:64, hh, 0:keys], got_pair(before(k, "it") + hh)[0:64, 0:keys]).then_inc(C["ia"], 1)

            def values(k, p):
                for t in range(NT[p] + PASSES[p][0]):
                    copy(vatt[:, t, :], got_pair(before(k, "it") + t)[:, 0:512]).then_inc(C["ia"], 1)

            def queries(k, p, t):
                b = got_pair(before(k, "it"))
                copy(qn.rearrange("p (a n) -> p a n", a=2), b.rearrange("p (a n) -> p a n", a=2)[:, :, 0:QL])\
                    .then_inc(C["ia"], 1)
                for i in range(2):
                    copy(QT[0:DQ, 4 * i:4 * i + 4, :], got_t(before(k, "tp") + i)[0:DQ, :, :]).then_inc(C["te"], 1)

            def scores(k, p, t, hh):
                keys = (NT[p] + PASSES[p][0]) * P
                b = got_pair(before(k, "it"))
                act.wait_ge(C["mx"], before(k, "mx") + 1)
                u = U0[p] + t
                if u:
                    act.wait_ge(C["td"], H * (u - 1) + hh + 1)
                nc.scalar.activation(Pn[:, hh % 2, 0:keys], b[:, 0:keys], ACT.Exp, scale=SCALE, bias=nb[:, hh % 2, :],
                                     accum_out=es[:, hh:hh + 1]).then_inc(C["ia"], 1)

            def head(k, p, t, hh):
                kt_n = NT[p] + PASSES[p][0]
                n = before(k, "tp")
                a = min(4, kt_n)
                copy(PT[:, hh % 2, 0:a, :], got_t(n)[:, 0:a, :]).then_inc(C["te"], 1)
                if kt_n > 4:
                    copy(PT[:, hh % 2, 4, :], got_t(n + 1)[:, 0, :]).then_inc(C["te"], 1)

            def gate_row(k):
                b = got_pair(before(k, "it"))
                if before(k, "id"):
                    act.wait_ge(C["id"], before(k, "id"))
                if before(k, "xr"):
                    act.wait_ge(C["xr"], before(k, "xr"))
                copy(gate[:, :], b).then_inc(C["ia"], 1)

            def output(k, p, t, step):
                if step:
                    return
                gate_row(k)
                for i in range(2):
                    copy(mT[:, 4 * i:4 * i + 4, :], got_t(before(k, "tp") + i)).then_inc(C["te"], 1)

            def peer_queries(k, p, t, step):
                if (step + 1) * WCH % 8:
                    return
                i = step * WCH // 8
                b = got_pair(before(k, "it"))
                copy(qpT[:, 8 * i:8 * i + 8, :], b.rearrange("p (a t) -> p a t", t=P)).then_inc(C["ia"], 1)

            def sub_key_scores(k, p, t):
                g, l = PASSES[p]
                act.wait_ge(s_out, 32 * (l + 1))
                for i in range(2):
                    b = got_pair(before(k, "it") + i)
                    copy(SS[:, 8 * i:8 * i + 8, :], b.rearrange("p (a k) -> p a k", k=NK)).then_inc(C["ia"], 1)

            def soft(k, u):
                act.wait_ge(C["tk"], u + 1)
                nc.scalar.activation(gw[:, u % 3, :, :], bs[:, :, :], ACT.Exp).then_inc(C["ge"], 1)

            def gelu(k, u):
                act.wait_ge(C["dot"], u + 1)
                nc.scalar.activation(gl[:, :], dot[:, :], ACT.Gelu).then_inc(C["gl"], 1)

            def sum_v(k, u, c):
                if c == 0:
                    act.wait_ge(C["wv"], u + 1)
                for i in range(CH):
                    n = before(k, "gv") + i
                    if n >= DR:
                        act.wait_ge(C["gv"], n - DR + 1)
                    copy(dgw[:, n % DR, :], ident[:, :], scale=wv[:, c * CH + i:c * CH + i + 1]).then_inc(C["dg"], 1)

            def finish(k, u):
                gate_row(k)

            def result(k, u):
                root(k, sty[:, 2:3], sty[:, 1:2])

            act.wait_ge(s_const, CONST + 16)
            nc.scalar.activation(cond[:, :, :], cond[:, :, :], ACT.Silu).then_inc(s_cond, 1)
            act.wait_ge(s_lbd, 1)
            nc.scalar.activation(lt[:, 0:2, :, :], lt[:, 0:2, :, :], ACT.Exp).then_inc(s_lbe, 1)
            do = {"norm": norm, "inp": project, "hg": recurrence, "hgfin": out_norm, "latn": latents, "latT": latents_T,
                  "kn": keys_T, "va": values, "q": queries, "sc": scores, "pv": head, "outp": output,
                  "wq": peer_queries, "score": sub_key_scores, "soft": soft, "gelu": gelu, "v": sum_v, "fin": finish,
                  "y": result}
            for k, step in enumerate(PLAN):
                if step[0] in do:
                    do[step[0]](k, *step[1:])

        @block.vector
        def _(dve):
            v = nc.vector
            linked = 0

            def link(ins):
                nonlocal linked
                linked += 1
                ins.then_inc(c_dve, 1)
                dve.wait_ge(c_dve, linked)

            def rms(k, src, junk, s, n):
                link(v.tensor_tensor_reduce(junk, src, src, 1.0, 0.0, ALU.mult, ALU.add, s[:, 0:1]))
                v.tensor_scalar(s[:, 1:2], s[:, 0:1], 1.0 / n, EPS, ALU.mult, ALU.add).then_inc(C["ms"], 1)
                dve.wait_ge(C["rt"], before(k, "rt") + 1)
                link(v.reciprocal(s[:, 3:4], s[:, 2:3]))

            def norm(k, p, t, which):
                g = PASSES[p][0]
                if before(k, "tp"):
                    dve.wait_ge(C["tp"], before(k, "tp"))
                rms(k, x[:, g + t, :], xn[:, :], st, D)
                v.tensor_scalar(xn[:, :], x[:, g + t, :], st[:, 3:4], None, ALU.mult).then_inc(C["xn"], 1)

            def forget(k, p, b):
                g, l = PASSES[p]
                t0, t1 = BATCHES[p][b]
                if b == 0:
                    if g:
                        dve.wait_ge(s_sw, 16 * n_small(p))
                    else:
                        if l:
                            dve.wait_ge(s_Sst, 16 * l)
                        link(v.memset(S[:, :, :, :], 0.0))
                dve.wait_ge(C["ia"], before(k, "ia"))
                for d in range(2):
                    for a in range(4):
                        f = sigq[:, 4 + 4 * d + a, t0 * P:t1 * P]
                        ins = v.tensor_scalar(f, f, omlb[:, d, l, a:a + 1], lb[:, d, l, a:a + 1], ALU.mult, ALU.add)
                link(ins)
                f = sigq[:, 4:12, t0 * P:t1 * P]
                link(v.tensor_scalar(f, f, FLOOR, None, ALU.max))

            def recurrence(k, p, d, t, step):
                first = PLACE["hg", p, d, t, 0]
                lv, it = before(first, "lv"), before(k, "it")
                cols = slice(t * P, (t + 1) * P)
                qt, ft = sigq[:, 0:4, cols], sigq[:, 4 + 4 * d:8 + 4 * d, cols]
                hi, lo = (1, 0) if d == 0 else (0, 1)
                def double(c):
                    e = c - 1 if d == 0 else 0
                    pv = Pt[:, :, :].rearrange("p g (n two c) -> p (g n) two c", two=2, c=c)
                    xv = Xt[:, :, :].rearrange("p g (n two c) -> p (g n) two c", two=2, c=c)
                    m = 4 * P // (2 * c)
                    link(v.tensor_tensor(xv[:, :, lo, :], xv[:, :, lo, :], pv[:, :, hi, e:e + 1].to_broadcast([P, m, c]),
                                         ALU.mult))
                    link(v.tensor_tensor(pv[:, :, hi, :], pv[:, :, hi, :], pv[:, :, lo, e:e + 1].to_broadcast([P, m, c]),
                                         ALU.mult))

                def operands(m):
                    n = lv + m
                    if m >= 2:
                        dve.wait_ge(C["it"], after(("hg", p, d, t, m - 2), "it"))
                    if m == 0:
                        link(v.reciprocal(KX[:, n % 2], Pt[:, :, :]))
                        link(v.tensor_tensor(KX[:, n % 2], KX[:, n % 2], Kt[:, :, :], ALU.mult))
                    else:
                        link(v.tensor_tensor(KX[:, n % 2], Xt[:, :, :], Kt[:, :, :], ALU.mult))
                    v.tensor_tensor(QP[:, n % 2], Pt[:, :, :], qt, ALU.mult).then_inc(C["lv"], 1)

                def merge(m):
                    dve.wait_ge(C["it"], it + 1)
                    for e in range(2):
                        src = pp[:, it % 2, 512 * e:512 * (e + 1)].rearrange("p (g t) -> p g t", t=P)
                        if m == 0:
                            ins = v.tensor_tensor(Asb[:, e], src, maskf[:, d, :].unsqueeze(1).to_broadcast([P, 4, P]),
                                                  ALU.mult)
                        else:
                            ins = v.copy_predicated(Asb[:, e], mk[:, d, m, :].unsqueeze(1).to_broadcast([P, 4, P]), src)
                        if e == 0:
                            link(ins)
                    ins.then_inc(C["id"], 1)
                    dve.wait_ge(C["id"], before(k, "id") + 1)

                if step == 0:
                    v.tensor_scalar(Kt[:, :, :], ft, -1.0, 1.0, ALU.mult, ALU.add)
                    v.tensor_copy(Pt[:, :, :], ft)
                    link(v.memset(Xt[:, :, :], 1.0))
                    double(1)
                    double(2)
                    operands(0)
                if step < LV - 1:
                    operands(step + 1)
                    dve.wait_ge(C["lv"], lv + step + 2)
                    merge(step)
                    if step < len(LEVELS):
                        double(LEVELS[step])
                    return
                dve.sem_inc(C["hgn"], 1)
                dve.wait_ge(C["o"], before(k, "o") + 1)
                e = P - 1 if d == 0 else 0
                link(v.tensor_tensor(S[:, d], S[:, d], Pt[:, :, e:e + 1].to_broadcast([P, 4, DK]), ALU.mult))
                n = it
                dve.wait_ge(C["it"], n + 1)
                ov = o[:, t, :].rearrange("p (g e n) -> p g e n", e=2, n=DK)
                for e in range(2):
                    src = pp[:, n % 2, 512 * e:512 * e + 256].rearrange("p (g n) -> p g n", n=DK)
                    if d == 0:
                        v.tensor_copy(ov[:, :, e, :], src)
                    else:
                        v.tensor_tensor(ov[:, :, e, :], src, ov[:, :, e, :], ALU.add)
                for e in range(2):
                    r = slice(64 * e, 64 * e + 64)
                    uv = pp[r, n % 2, 256:512].rearrange("p (g n) -> p g n", n=DK)
                    link(v.tensor_tensor(S[r, d], uv, S[r, d], ALU.add))
                dve.sem_inc(C["S"], 1)
                dve.sem_inc(C["id"], 1)

            def out_norm(k, p, t):
                l = PASSES[p][1]
                if before(k, "tp"):
                    dve.wait_ge(C["tp"], before(k, "tp"))
                ov = o[:, t, :].rearrange("p (h n) -> p h n", n=DK)
                sq = xn[:, 0:512].rearrange("p (h n) -> p h n", n=DK)
                link(v.tensor_tensor(sq, ov, ov, ALU.mult))
                link(v.tensor_reduce(st8[:, 0, :], sq, AX.X, ALU.add))
                v.tensor_scalar(st8[:, 1, :], st8[:, 0, :], 1.0 / DK, EPS, ALU.mult, ALU.add).then_inc(C["ms"], 1)
                dve.wait_ge(C["rt"], before(k, "rt") + 1)
                link(v.reciprocal(st8[:, 3, :], st8[:, 2, :]))
                link(v.tensor_tensor(ov, ov, st8[:, 3, :].unsqueeze(2).to_broadcast([P, H, DK]), ALU.mult))
                link(v.tensor_tensor(ov, ov, hrow[:, l, :].unsqueeze(1).to_broadcast([P, H, DK]), ALU.mult))
                v.tensor_tensor(o[:, t, :], o[:, t, :], GT[:, t, :], ALU.mult).then_inc(C["hg"], 1)

            def rotate(vec, n, cos, sin):
                x1, x2 = vec[:, :, 0, :], vec[:, :, 1, :]
                tmp = [rt[:, i, 0:n * 8].rearrange("p (a b) -> p a b", b=8) for i in range(4)]
                v.tensor_tensor(tmp[0], x1, cos, ALU.mult)
                v.tensor_tensor(tmp[1], x2, sin, ALU.mult)
                v.tensor_tensor(tmp[2], x1, sin, ALU.mult)
                link(v.tensor_tensor(tmp[3], x2, cos, ALU.mult))
                v.tensor_tensor(x1, tmp[0], tmp[1], ALU.subtract)
                return v.tensor_tensor(x2, tmp[2], tmp[3], ALU.add)

            def latents(k, p):
                g, nt = PASSES[p][0], NT[p]
                dve.wait_ge(s_sw, 16 * n_small(p))
                link(v.memset(st8[:, 1, :], 1.0))
                for t in range(nt):
                    link(v.tensor_tensor_reduce(xn[:, 0:QL], cq[:, t, :], cq[:, t, :], 1.0 / QL, EPS, ALU.mult, ALU.add,
                                                st8[:, 1, t:t + 1]))
                    ins = v.tensor_tensor_reduce(xn[:, 0:KVL], ckv[:, g + t, :], ckv[:, g + t, :], 1.0 / KVL, EPS,
                                                 ALU.mult, ALU.add, st8[:, 1, 4 + t:5 + t])
                    if t + 1 < nt:
                        link(ins)
                ins.then_inc(C["ms"], 1)
                dve.wait_ge(C["rt"], before(k, "rt") + 1)
                link(v.reciprocal(st8[:, 3, :], st8[:, 2, :]))
                for t in range(nt):
                    v.scalar_tensor_tensor(cq[:, t, :], cq[:, t, :], st8[:, 3, t:t + 1], qrow[:, :], ALU.mult, ALU.mult)
                    ins = v.scalar_tensor_tensor(ckv[:, g + t, :], ckv[:, g + t, :], st8[:, 3, 4 + t:5 + t], kvrow[:, :],
                                                 ALU.mult, ALU.mult)
                if g:
                    link(ins)
                    for a in range(nt):
                        vec = kpe[:, 1 + a, :].rearrange("p (x two n) -> p x two n", x=2, two=2)
                        ins = rotate(vec, 2, rope[:, 0, a, :].rearrange("p (x n) -> p x n", x=2),
                                     rope[:, 1, a, :].rearrange("p (x n) -> p x n", x=2))
                        if a + 1 < nt:
                            link(ins)
                ins.then_inc(C["cn"], 1)

            def queries(k, p, t):
                if not PASSES[p][0]:
                    return
                dve.wait_ge(C["tp"], before(k, "tp"))
                dve.wait_ge(C["ia"], before(k, "ia") + 1)
                qv = qn.rearrange("p (h n) -> p h n", n=DQ)
                for ax in range(2):
                    vec = qv[:, :, 64 + 16 * ax:80 + 16 * ax].rearrange("p h (two n) -> p h two n", two=2)
                    cs = [rope[:, i, t, 8 * ax:8 * ax + 8].unsqueeze(1).to_broadcast([P, H, 8]) for i in range(2)]
                    ins = rotate(vec, 8, cs[0], cs[1])
                    if ax == 0:
                        link(ins)
                ins.then_inc(C["qr"], 1)

            def scores(k, p, t, hh):
                keys = (NT[p] + PASSES[p][0]) * P
                n = before(k, "it")
                dve.wait_ge(C["it"], n + 1)
                dve.wait_ge(C["ia"], before(k, "ia") - 1)
                link(v.tensor_reduce(mx[:, hh % 2, :], pp[:, n % 2, 0:keys], AX.X, ALU.max))
                v.tensor_scalar(nb[:, hh % 2, :], mx[:, hh % 2, :], -SCALE, None, ALU.mult).then_inc(C["mx"], 1)

            def head(k, p, t, hh):
                bank = (before(k + 1, "tp") - 1) % 2
                dve.wait_ge(C["ia"], after(("sc", p, t, hh), "ia"))
                link(v.reciprocal(ri[:, hh:hh + 1], es[:, hh:hh + 1]))
                dve.wait_ge(C["pv"], before(k, "pv") + 1)
                v.tensor_scalar(att[:, t, hh * DK:(hh + 1) * DK], tb[:, bank, 256:256 + DK], ri[:, hh:hh + 1], None,
                                ALU.mult).then_inc(C["td"], 1)

            def output(k, p, t, step):
                g = PASSES[p][0]
                if step == 0:
                    dve.wait_ge(C["ia"], before(k, "ia") + 1)
                if step < N_OUT // WCH - 1:
                    return
                n = before(k, "it")
                dve.wait_ge(C["it"], n + 1)
                link(v.tensor_tensor(xn[:, :], pp[:, n % 2, :], gate[:, :], ALU.mult))
                v.tensor_tensor(x[:, g + t, :], x[:, g + t, :], xn[:, :], ALU.add).then_inc(C["id"], 1)
                dve.wait_ge(C["id"], before(k, "id") + 1)

            def top16(vals, idx, src, scratch):
                link(v.max(vals[:, 0:8], src))
                v.max_index(idx[:, 0:8], vals[:, 0:8], src)
                link(v.match_replace(scratch, vals[:, 0:8], src, -3.0e38))
                link(v.max(vals[:, 8:16], scratch))
                link(v.max_index(idx[:, 8:16], vals[:, 8:16], scratch))

            def topk(k, u, hh):
                l = 0 if u < U0[2] else 1
                if hh == 0:
                    dve.wait_ge(C["ia"], before(k, "ia"))
                    if u >= 3:
                        dve.wait_ge(C["gv"], H * TOPK * (u - 2))
                for s in range(2):
                    top16(v16[:, s], i16[:, s], SS[:, 2 * hh + s, :], cand[:, 1, 0:NK])
                v.tensor_copy(i16f[:, :, :], i16[:, :, :])
                cv = cand[:, 0, :].rearrange("p (a b) -> p a b", b=TOPK)
                link(v.tensor_tensor(cv, v16[:, 0, :].unsqueeze(2).to_broadcast([P, TOPK, TOPK]),
                                     v16[:, 1, :].unsqueeze(1).to_broadcast([P, TOPK, TOPK]), ALU.add))
                top16(bs[:, hh], pos, cand[:, 0, :], cand[:, 1, :])
                v.tensor_scalar(ab[:, 0, :], pos[:, :], 4, None, ALU.logical_shift_right)
                link(v.tensor_scalar(ab[:, 1, :], pos[:, :], TOPK - 1, None, ALU.bitwise_and))
                link(v.tensor_copy(abf[:, :, :], ab[:, :, :]))
                hot = [cand[:, s, :].rearrange("p (a b) -> p a b", b=TOPK) for s in range(2)]
                for op in range(3):
                    for s in range(2):
                        if op == 0:
                            ins = v.tensor_tensor(hot[s], abf[:, s, :].unsqueeze(2).to_broadcast([P, TOPK, TOPK]),
                                                  iota16[:, :].unsqueeze(1).to_broadcast([P, TOPK, TOPK]), ALU.is_equal)
                        elif op == 1:
                            ins = v.tensor_tensor(hot[s], hot[s], i16f[:, s, :].unsqueeze(1).to_broadcast([P, TOPK, TOPK]),
                                                  ALU.mult)
                        else:
                            ins = v.tensor_reduce(pick[:, s, :], hot[s], AX.X, ALU.add)
                    link(ins)
                link(v.tensor_scalar(pick[:, 0, :], pick[:, 0, :], float(NK), float(l * EXPERTS), ALU.mult, ALU.add))
                link(v.tensor_tensor(eidx[:, u % 3, hh * TOPK:(hh + 1) * TOPK], pick[:, 0, :], pick[:, 1, :], ALU.add))

            def soft(k, u):
                link(v.tensor_copy(gs[:, 0, :], bs[:, :, 0]))
                v.tensor_tensor(bs[:, :, :], bs[:, :, :], gs[:, 0, :].unsqueeze(2).to_broadcast([P, H, TOPK]),
                                ALU.subtract).then_inc(C["tk"], 1)
                dve.wait_ge(C["ge"], u + 1)
                link(v.tensor_reduce(gs[:, 0, :], gw[:, u % 3, :, :], AX.X, ALU.add))
                link(v.reciprocal(gs[:, 1, :], gs[:, 0, :]))
                link(v.tensor_tensor(gw[:, u % 3, :, :], gw[:, u % 3, :, :],
                                     gs[:, 1, :].unsqueeze(2).to_broadcast([P, H, TOPK]), ALU.mult))

            def dots(k, u, c):
                if c == 0:
                    p = max(q for q in range(4) if U0[q] <= u)
                    dve.wait_ge(C["te"], after(("norm", p, u - U0[p], 1), "te"))
                for i in range(CH):
                    rows = landed(dve, "peer_u", u, c * CH + i)
                    n = c * CH + i
                    v.tensor_tensor_reduce(rows, rows, h2[:, u % 2, :], 1.0, 0.0, ALU.mult, ALU.add, dot[:, n:n + 1])\
                        .then_inc(C["gu"], 1)

            def gelu(k, u):
                dve.wait_ge(C["gu"], H * TOPK * (u + 1))
                dve.sem_inc(C["dot"], 1)
                dve.wait_ge(C["gl"], u + 1)
                v.tensor_tensor(wv[:, :], gl[:, :], gw[:, u % 3, :, :].rearrange("p h k -> p (h k)"), ALU.mult)\
                    .then_inc(C["wv"], 1)

            def finish(k, u):
                p = max(q for q in range(4) if U0[q] <= u)
                xt = x[:, PASSES[p][0] + u - U0[p], :]
                dve.wait_ge(C["gv"], H * TOPK * (u + 1))
                dve.wait_ge(C["ia"], before(k, "ia") + 1)
                link(v.tensor_tensor(acc[:, :], acc[:, :], gate[:, :], ALU.mult))
                v.tensor_tensor(xt, xt, acc[:, :], ALU.add).then_inc(C["xr"], 1)
                dve.wait_ge(C["xr"], u + 1)

            def result(k, u):
                i = u - (NU - 5)
                dve.wait_ge(s_frow, 16)
                if i >= 2:
                    dve.wait_ge(s_yst[i % 2], 16 * (i // 2))
                out = yt[:, i % 2, :]
                rms(k, x[:, i, :], out, sty, D)
                v.scalar_tensor_tensor(out, x[:, i, :], sty[:, 3:4], frow, ALU.mult, ALU.mult).then_inc(C["y"], 1)

            def modulation(k, l, i):
                n = before(k, "it")
                dve.wait_ge(C["it"], n + 1)
                js = slice(i * ADA, (i + 1) * ADA)
                v.tensor_tensor(mods[:, l, js, :], pp[:, n % 2, 0:2 * ADA].rearrange("p (j c) -> p j c", c=2),
                                bada[:, l, js].unsqueeze(2).to_broadcast([P, ADA, 2]), ALU.add).then_inc(C["id"], 1)

            def modulation_end(k, l):
                dve.wait_ge(C["id"], before(k, "id"))
                for which in range(2):
                    a = Am[:, l, which, :, :]
                    link(v.tensor_scalar(a, mods[:, l, (3 * which + 1) * KC:(3 * which + 2) * KC, :], 1.0, None, ALU.add))
                    ins = v.tensor_tensor(a, a, nrm[:, l, which, :].unsqueeze(2).to_broadcast([P, KC, 2]), ALU.mult)
                    if which == 0:
                        link(ins)
                ins.then_inc(C["mods"], 1)

            dve.wait_ge(s_const, CONST + 16)
            link(v.tensor_copy(mk[:, :, :, :], U[:, 0:2 * 6 * P].bitcast(I32).rearrange("p (d m t) -> p d m t", d=2, t=P)))
            top = lt[:, 2]
            link(v.tensor_tensor(top, lbl[:, :, 0, :], lbl[:, :, 1, :], ALU.max))
            for i in range(DEPTH):
                ins = v.tensor_tensor(lt[:, i], lbl[:, :, i, :], top, ALU.subtract)
                if i == 0:
                    link(ins)
            ins.then_inc(s_lbd, 1)
            dve.wait_ge(s_lbe, 1)
            link(v.tensor_tensor(lt[:, 3], lt[:, 0], lt[:, 1], ALU.add))
            link(v.reciprocal(lt[:, 3], lt[:, 3]))
            link(v.tensor_tensor(lt[:, 0], lt[:, 0], lt[:, 3], ALU.mult))
            link(v.tensor_tensor(lt[:, 1], lt[:, 1], lt[:, 3], ALU.mult))
            link(v.tensor_tensor(lb[:, :, 0, :], lt[:, 0], lt[:, 0], ALU.subtract))
            link(v.tensor_tensor(lt[:, 2], lt[:, 0], lt[:, 1], ALU.add))
            link(v.tensor_tensor(lb[:, :, 1, :], lt[:, 2], lt[:, 0], ALU.subtract))
            link(v.tensor_scalar(omlb[:, :, :, :], lb[:, :, :, :], -1.0, 1.0, ALU.mult, ALU.add))
            do = {"norm": norm, "fgate": forget, "hg": recurrence, "hgfin": out_norm, "latn": latents, "q": queries,
                  "sc": scores, "pv": head, "outp": output, "topk": topk, "soft": soft, "u": dots, "gelu": gelu,
                  "fin": finish, "y": result, "ada": modulation, "adafin": modulation_end}
            for k, step in enumerate(PLAN):
                if step[0] in do:
                    do[step[0]](k, *step[1:])


def kernel(**inputs):
    import concourse.bacc as _bacc
    from concourse.bass_utils import run_bass_kernel_spmd as _run

    f = {k: np.ascontiguousarray(v) for k, v in inputs.items()}

    def tiles(w, n):
        return np.ascontiguousarray(w.reshape(DEPTH, KC, P, n, P).transpose(0, 3, 2, 1, 4))

    def rows(a):
        return np.ascontiguousarray(np.broadcast_to(a[None], (P,) + a.shape))

    inv = (1.0 / (10000.0 ** (np.arange(0, 16, 2, dtype=np.float32) / np.float32(16)))).astype(np.float32)
    tok = np.arange(DEC)
    ang = np.concatenate([(tok // 64).astype(np.float32)[:, None] * inv,
                          (tok % 64).astype(np.float32)[:, None] * inv], -1).astype(np.float32)
    table = np.stack([np.cos(ang), np.sin(ang)]).astype(np.float32)
    mk = masks()
    n_main = (N_IN - 1) * P
    arrays = {
        "ident": np.eye(P, dtype=np.float32),
        "masks": np.ascontiguousarray(mk.transpose(2, 0, 1, 3)),
        "maskf": np.ascontiguousarray(mk[:, 0].transpose(1, 0, 2)).astype(np.float32),
        "rope": np.ascontiguousarray(table.reshape(2, 4, P, 16).transpose(2, 0, 1, 3)),
        "cond": np.ascontiguousarray(np.stack([f["c_ctx"], f["c"][0]]).reshape(2, KC, P).transpose(2, 1, 0)),
        "b_ada": np.ascontiguousarray(f["b_ada"].reshape(DEPTH, N_ADA, P).transpose(2, 0, 1)),
        "nrm": np.ascontiguousarray(np.stack([f["norm_mix"], f["norm_ffn"]], 1).reshape(DEPTH, 2, KC, P)
                                    .transpose(3, 0, 1, 2)),
        "lbl": np.ascontiguousarray(f["hgrn_lb_logits"].reshape(2, DEPTH, 4, P).transpose(3, 0, 1, 2)),
        "x": np.ascontiguousarray(np.concatenate([f["x_prompt"][0], f["x_sample"][0]]).reshape(5, P, D)
                                  .transpose(1, 0, 2)),
        "qrow": np.ascontiguousarray(np.broadcast_to(f["mla_q_norm"][:, None], (DEPTH, P, QL))),
        "kvrow": np.ascontiguousarray(np.broadcast_to(f["mla_kv_norm"][:, None], (DEPTH, P, KVL))),
        "hrow": rows(f["hgrn_norm"]),
        "frow": rows(f["final_norm"]),
        "w_ada": tiles(f["w_ada"], N_ADA),
        "w_in": tiles(np.ascontiguousarray(f["w_in"][:, :, :n_main]), N_IN - 1),
        "w_in_tail": np.ascontiguousarray(f["w_in"][:, :, n_main:].reshape(DEPTH, KC, P, ROPE).transpose(0, 2, 1, 3)),
        "w_out": tiles(f["w_out"], N_OUT),
        "w_q": tiles(f["peer_wq"], N_WQ),
        "wqb": np.ascontiguousarray(f["mla_wqb"].reshape(DEPTH, 3, P, H * DQ).transpose(0, 2, 1, 3)),
        "wkvb": np.ascontiguousarray(f["mla_wkvb"].reshape(DEPTH, 2, P, H * P).transpose(0, 2, 1, 3)),
        "keys": np.ascontiguousarray(f["peer_keys"].transpose(0, 4, 2, 1, 3).reshape(DEPTH, P, 2 * H, NK)),
        "cache_ckv": f["cache_ckv"][0], "cache_kpe": f["cache_kpe"][0],
        "state": np.ascontiguousarray(f["state_hgrn"][0].reshape(DEPTH, 2, 4, P, DK).transpose(0, 3, 1, 2, 4)),
        "peer_u": f["peer_u"].reshape(DEPTH * EXPERTS, D), "peer_v": f["peer_v"].reshape(DEPTH * EXPERTS, D),
    }
    outs = {"y": (5, P, D), "ckv": (DEPTH, P, KVL), "kpe": (DEPTH, P, ROPE), "state": (DEPTH, P, 2, 4, DK)}
    nc = _bacc.Bacc("TRN2", target_bir_lowering=False, num_devices=1)
    A = {k: nc.dram_tensor(f"in_{k}", v.shape, mybir.dt.from_np(v.dtype), kind="ExternalInput").ap()
         for k, v in arrays.items()}
    O = {k: nc.dram_tensor(f"out_{k}", s, F32, kind="ExternalOutput").ap() for k, s in outs.items()}
    build(nc, A, O)
    r = _run(nc, [{f"in_{k}": v for k, v in arrays.items()}], core_ids=[0]).results[0]
    y = r["out_y"].reshape(5 * P, D)
    state = r["out_state"].transpose(0, 2, 3, 1, 4).reshape(1, DEPTH, 2, H, DK, DK)
    return (y[None, :SEQ], y[None, SEQ:], r["out_ckv"][None], r["out_kpe"][None], state)
```
